# Optimizing a Trainium2 kernel written in Bass

```python
import jax, jax.numpy as jnp
from jax import lax
import numpy as np

D_MODEL = 1024
BATCH = 1
SEQ = 128
DEPTH = 1
DEC_BATCH = 1
DEC_SEQ = 256
PAST_LEN = 128

GRID_W = 64
ATTN_HEADS = 8
KV_HEADS = 2
HEAD_DIM = 64
ATTN_WIDTH = ATTN_HEADS * HEAD_DIM
KV_WIDTH = KV_HEADS * HEAD_DIM
ROPE_THETA = 10000.0
Q_BLOCK = 128
GLA_HEADS = 4
GLA_DK = 64
GLA_DV = 128
GLA_K_WIDTH = GLA_HEADS * GLA_DK
GLA_V_WIDTH = GLA_HEADS * GLA_DV
GLA_GATE_RANK = 16
GLA_TAU = 16.0
GLA_CHUNK = 64
N_BRANCHES = 2
IN_WIDTHS = (ATTN_WIDTH, KV_WIDTH, KV_WIDTH, GLA_K_WIDTH, GLA_K_WIDTH, GLA_V_WIDTH, GLA_V_WIDTH,
             2 * GLA_GATE_RANK, N_BRANCHES * D_MODEL)
IN_TOTAL = (ATTN_WIDTH + 2 * KV_WIDTH + 2 * GLA_K_WIDTH + 2 * GLA_V_WIDTH
            + 2 * GLA_GATE_RANK + N_BRANCHES * D_MODEL)
N_GROUPS = 4
EXPERTS_PER_GROUP = 8
N_EXPERTS = N_GROUPS * EXPERTS_PER_GROUP
D_EXPERT = 256
TOP_K_INNER = 2
DEEPNORM_ALPHA = (2.0 * DEPTH) ** 0.25
DEEPNORM_BETA = (8.0 * DEPTH) ** -0.25
LN_EPS = 1e-6
RMS_EPS = 1e-6

kernel_name = "hybrid_gqa_gla_hmoe_diffusion_step"

def _ln_f32(x):
    xf = x.astype(jnp.float32)
    mu = jnp.mean(xf, axis=-1, keepdims=True)
    var = jnp.mean(jnp.square(xf - mu), axis=-1, keepdims=True)
    return (xf - mu) * lax.rsqrt(var + LN_EPS)

def ln_plain(x):
    return _ln_f32(x).astype(x.dtype)

def ln_affine(x, g, b):
    return (_ln_f32(x) * g.astype(jnp.float32) + b.astype(jnp.float32)).astype(x.dtype)

def rms_norm(x, g):
    xf = x.astype(jnp.float32)
    y = xf * lax.rsqrt(jnp.mean(jnp.square(xf), axis=-1, keepdims=True) + RMS_EPS)
    return (y * g.astype(jnp.float32)).astype(x.dtype)

def rope_1d(x, pos):
    half = x.shape[-1] // 2
    inv = ROPE_THETA ** (-jnp.arange(half, dtype=jnp.float32) / half)
    ang = pos[:, None] * inv[None, :]
    cos = jnp.cos(ang)[None, :, None, :]
    sin = jnp.sin(ang)[None, :, None, :]
    x1, x2 = x[..., :half], x[..., half:]
    return jnp.concatenate([x1 * cos - x2 * sin, x2 * cos + x1 * sin], axis=-1)

def axial_rope(x):
    n = x.shape[1]
    rows = n // GRID_W
    row = jnp.repeat(jnp.arange(rows, dtype=jnp.float32), GRID_W)
    col = jnp.tile(jnp.arange(GRID_W, dtype=jnp.float32), rows)
    half = HEAD_DIM // 2
    xf = x.astype(jnp.float32)
    out = jnp.concatenate([rope_1d(xf[..., :half], row), rope_1d(xf[..., half:], col)], axis=-1)
    return out.astype(x.dtype)

def block_attention(q, k, v):
    b, s, h, hd = q.shape
    kv = k.shape[2]
    g = h // kv
    nb = s // Q_BLOCK
    kf = k.astype(jnp.float32)
    vf = v.astype(jnp.float32)
    qb = q.astype(jnp.float32).reshape(b, nb, Q_BLOCK, kv, g, hd).transpose(1, 0, 2, 3, 4, 5)
    scale = hd ** -0.5

    def one_block(qblk):
        sc = jnp.einsum('bqkgd,btkd->bkgqt', qblk, kf) * scale
        p = jax.nn.softmax(sc, axis=-1)
        return jnp.einsum('bkgqt,btkd->bqkgd', p, vf)

    ob = lax.map(one_block, qb)
    return ob.transpose(1, 0, 2, 3, 4, 5).reshape(b, s, h * hd).astype(q.dtype)

def gla_chunked(q, k, v, logg, s0):
    b, n, h, dk = q.shape
    dv = v.shape[-1]
    nc = n // GLA_CHUNK

    def chunks(t):
        return t.reshape(b, nc, GLA_CHUNK, h, t.shape[-1]).transpose(1, 0, 3, 2, 4)

    mask = jnp.tril(jnp.ones((GLA_CHUNK, GLA_CHUNK), dtype=bool))

    def step(state, inp):
        qc, kc, vc, gc = inp
        cum = jnp.cumsum(gc, axis=2)
        q_t = qc * jnp.exp(cum)
        k_t = kc * jnp.exp(-cum)
        a = jnp.where(mask, jnp.einsum('bhcd,bhsd->bhcs', q_t, k_t), 0.0)
        o = jnp.einsum('bhcd,bhde->bhce', q_t, state) + jnp.einsum('bhcs,bhse->bhce', a, vc)
        last = cum[:, :, -1:, :]
        new_state = (jnp.exp(last[:, :, 0, :])[..., None] * state
                     + jnp.einsum('bhsd,bhse->bhde', kc * jnp.exp(last - cum), vc))
        return new_state, o

    s_fin, o = lax.scan(step, s0, (chunks(q), chunks(k), chunks(v), chunks(logg)))
    o = o.transpose(1, 0, 3, 2, 4).reshape(b, n, h, dv)
    return o, s_fin

def hier_moe(h, lp):
    b, n, d = h.shape
    t = h.reshape(b * n, d)
    lg = (t @ lp['router_group_w'] + lp['router_group_b']).astype(jnp.float32)
    pg = jax.nn.softmax(lg, axis=-1)
    pg_top, g_idx = lax.top_k(pg, 1)
    le = (t @ lp['router_expert_w'] + lp['router_expert_b']).astype(jnp.float32)
    le = le.reshape(b * n, N_GROUPS, EXPERTS_PER_GROUP)
    le_sel = jnp.einsum('tg,tge->te', jax.nn.one_hot(g_idx[:, 0], N_GROUPS, dtype=jnp.float32), le)
    top_v, top_i = lax.top_k(le_sel, TOP_K_INNER)
    w = jax.nn.softmax(top_v, axis=-1) * pg_top
    e_idx = g_idx * EXPERTS_PER_GROUP + top_i
    comb = jnp.einsum('tk,tke->te', w, jax.nn.one_hot(e_idx, N_EXPERTS, dtype=jnp.float32)).astype(t.dtype)
    y = jnp.zeros_like(t)
    for e in range(N_EXPERTS):
        hid = jax.nn.silu(t @ lp['exp_w_gate'][e]) * (t @ lp['exp_w_up'][e])
        y = y + comb[:, e:e + 1] * (hid @ lp['exp_w_down'][e])
    return y.reshape(b, n, d)

def trunk_layer(x, mod, lp, latent, ctx_k, ctx_v, s0_fwd, s0_bwd):
    b, n, _ = x.shape
    f32 = jnp.float32
    sh1, sc1, g1, sh2, sc2, g2 = jnp.split(mod, 6, axis=-1)
    h = ln_plain(x) * (1 + sc1) + sh1
    offs = [int(o) for o in np.cumsum(IN_WIDTHS)[:-1]]
    q_a, k_a, v_a, q_g, k_g, v_g, r_g, lr, mg = jnp.split(h @ lp['w_in'], offs, axis=-1)

    q_a = rms_norm(q_a.reshape(b, n, ATTN_HEADS, HEAD_DIM), lp['q_norm'])
    k_a = rms_norm(k_a.reshape(b, n, KV_HEADS, HEAD_DIM), lp['k_norm'])
    v_a = v_a.reshape(b, n, KV_HEADS, HEAD_DIM)
    if latent:
        keys = jnp.concatenate([axial_rope(k_a), ctx_k.astype(k_a.dtype)], axis=1)
        vals = jnp.concatenate([v_a, ctx_v.astype(v_a.dtype)], axis=1)
        q_a = axial_rope(q_a)
    else:
        keys, vals = k_a, v_a
    attn = block_attention(q_a, keys, vals)

    qg = q_g.reshape(b, n, GLA_HEADS, GLA_DK).astype(f32) * (GLA_DK ** -0.5)
    kg = k_g.reshape(b, n, GLA_HEADS, GLA_DK).astype(f32)
    vg = v_g.reshape(b, n, GLA_HEADS, GLA_DV).astype(f32)
    z = jnp.einsum('bnjr,jrd->bnjd', lr.reshape(b, n, 2, GLA_GATE_RANK), lp['gla_w_gate']) + lp['gla_b_gate']
    logg = (jax.nn.log_sigmoid(z.astype(f32)) / GLA_TAU).reshape(b, n, 2, GLA_HEADS, GLA_DK)
    o_f, s_f = gla_chunked(qg, kg, vg, logg[:, :, 0], s0_fwd.astype(f32))
    o_b, s_b = gla_chunked(jnp.flip(qg, axis=1), jnp.flip(kg, axis=1), jnp.flip(vg, axis=1),
                           jnp.flip(logg[:, :, 1], axis=1), s0_bwd.astype(f32))
    o = rms_norm(o_f + jnp.flip(o_b, axis=1), lp['gla_norm']).astype(h.dtype).reshape(b, n, GLA_V_WIDTH)
    gla = o * jax.nn.silu(r_g)

    gates = jax.nn.sigmoid(mg.reshape(b, n, N_BRANCHES, D_MODEL))
    merged = gates[:, :, 0] * (attn @ lp['w_br_attn']) + gates[:, :, 1] * (gla @ lp['w_br_gla'])
    x = ln_affine(DEEPNORM_ALPHA * x + g1 * (merged @ lp['w_out']), lp['ln1_g'], lp['ln1_b'])

    h2 = ln_plain(x) * (1 + sc2) + sh2
    x = ln_affine(DEEPNORM_ALPHA * x + g2 * hier_moe(h2, lp), lp['ln2_g'], lp['ln2_b'])
    return x, k_a, v_a, s_f.astype(x.dtype), s_b.astype(x.dtype)

def setup_inputs(seed: int = 0) -> dict:
    key = jax.random.key(seed)
    ks = jax.random.split(key, 32)

    def nrm(k, shape, scale):
        return jax.random.normal(k, shape, jnp.float32) * scale

    D = D_MODEL
    return {
        'x_prompt': nrm(ks[0], (BATCH, SEQ, D), 1.0),
        'x_sample': nrm(ks[1], (DEC_BATCH, DEC_SEQ, D), 1.0),
        'cache_k': nrm(ks[2], (DEC_BATCH, DEPTH, PAST_LEN, KV_HEADS, HEAD_DIM), 1.0),
        'cache_v': nrm(ks[3], (DEC_BATCH, DEPTH, PAST_LEN, KV_HEADS, HEAD_DIM), 1.0),
        'state_gla_fwd': nrm(ks[4], (DEC_BATCH, DEPTH, GLA_HEADS, GLA_DK, GLA_DV), 1.0),
        'state_gla_bwd': nrm(ks[5], (DEC_BATCH, DEPTH, GLA_HEADS, GLA_DK, GLA_DV), 1.0),
        'c': nrm(ks[6], (DEC_BATCH, D), 1.0),
        'c_ctx': nrm(ks[7], (D,), 1.0),
        'w_ada': nrm(ks[8], (DEPTH, D, 6 * D), 0.5 * D ** -0.5),
        'b_ada': nrm(ks[9], (DEPTH, 6 * D), 0.02),
        'w_in': nrm(ks[10], (DEPTH, D, IN_TOTAL), D ** -0.5),
        'q_norm': 1.0 + nrm(ks[11], (DEPTH, HEAD_DIM), 0.02),
        'k_norm': 1.0 + nrm(ks[12], (DEPTH, HEAD_DIM), 0.02),
        'gla_w_gate': nrm(ks[13], (DEPTH, 2, GLA_GATE_RANK, GLA_K_WIDTH), GLA_GATE_RANK ** -0.5),
        'gla_b_gate': nrm(ks[14], (DEPTH, 2, GLA_K_WIDTH), 0.1),
        'gla_norm': 1.0 + nrm(ks[15], (DEPTH, GLA_DV), 0.02),
        'w_br_attn': nrm(ks[16], (DEPTH, ATTN_WIDTH, D), ATTN_WIDTH ** -0.5),
        'w_br_gla': nrm(ks[17], (DEPTH, GLA_V_WIDTH, D), GLA_V_WIDTH ** -0.5),
        'w_out': nrm(ks[18], (DEPTH, D, D), DEEPNORM_BETA * D ** -0.5),
        'ln1_g': 1.0 + nrm(ks[19], (DEPTH, D), 0.02),
        'ln1_b': nrm(ks[20], (DEPTH, D), 0.02),
        'router_group_w': nrm(ks[21], (DEPTH, D, N_GROUPS), D ** -0.5),
        'router_group_b': nrm(ks[22], (DEPTH, N_GROUPS), 0.01),
        'router_expert_w': nrm(ks[23], (DEPTH, D, N_EXPERTS), D ** -0.5),
        'router_expert_b': nrm(ks[24], (DEPTH, N_EXPERTS), 0.01),
        'exp_w_gate': nrm(ks[25], (DEPTH, N_EXPERTS, D, D_EXPERT), D ** -0.5),
        'exp_w_up': nrm(ks[26], (DEPTH, N_EXPERTS, D, D_EXPERT), D ** -0.5),
        'exp_w_down': nrm(ks[27], (DEPTH, N_EXPERTS, D_EXPERT, D), DEEPNORM_BETA * D_EXPERT ** -0.5),
        'ln2_g': 1.0 + nrm(ks[28], (DEPTH, D), 0.02),
        'ln2_b': nrm(ks[29], (DEPTH, D), 0.02),
    }

def reference(x_prompt, x_sample, cache_k, cache_v, state_gla_fwd, state_gla_bwd, c, c_ctx,
              w_ada, b_ada, w_in, q_norm, k_norm, gla_w_gate, gla_b_gate, gla_norm,
              w_br_attn, w_br_gla, w_out, ln1_g, ln1_b, router_group_w, router_group_b,
              router_expert_w, router_expert_b, exp_w_gate, exp_w_up, exp_w_down, ln2_g, ln2_b):
    b_ctx = x_prompt.shape[0]
    zero_state = jnp.zeros((b_ctx, GLA_HEADS, GLA_DK, GLA_DV), jnp.float32)
    x_ctx = x_prompt
    x_lat = x_sample
    ks_new, vs_new, sf_new, sb_new = [], [], [], []
    for l in range(DEPTH):
        lp = {
            'w_in': w_in[l], 'q_norm': q_norm[l], 'k_norm': k_norm[l],
            'gla_w_gate': gla_w_gate[l], 'gla_b_gate': gla_b_gate[l], 'gla_norm': gla_norm[l],
            'w_br_attn': w_br_attn[l], 'w_br_gla': w_br_gla[l], 'w_out': w_out[l],
            'ln1_g': ln1_g[l], 'ln1_b': ln1_b[l],
            'router_group_w': router_group_w[l], 'router_group_b': router_group_b[l],
            'router_expert_w': router_expert_w[l], 'router_expert_b': router_expert_b[l],
            'exp_w_gate': exp_w_gate[l], 'exp_w_up': exp_w_up[l], 'exp_w_down': exp_w_down[l],
            'ln2_g': ln2_g[l], 'ln2_b': ln2_b[l],
        }
        mod_ctx = (jax.nn.silu(c_ctx) @ w_ada[l] + b_ada[l])[None, None, :]
        x_ctx, k_l, v_l, sf_l, sb_l = trunk_layer(x_ctx, mod_ctx, lp, False, None, None, zero_state, zero_state)
        ks_new.append(k_l)
        vs_new.append(v_l)
        sf_new.append(sf_l)
        sb_new.append(sb_l)
        mod_lat = (jax.nn.silu(c) @ w_ada[l] + b_ada[l])[:, None, :]
        x_lat, _, _, _, _ = trunk_layer(x_lat, mod_lat, lp, True, cache_k[:, l], cache_v[:, l],
                                        state_gla_fwd[:, l], state_gla_bwd[:, l])
    new_cache_k = jnp.stack(ks_new, axis=1)
    new_cache_v = jnp.stack(vs_new, axis=1)
    new_state_gla_fwd = jnp.stack(sf_new, axis=1)
    new_state_gla_bwd = jnp.stack(sb_new, axis=1)
    return (x_ctx, x_lat, new_cache_k, new_cache_v, new_state_gla_fwd, new_state_gla_bwd)


_drawn_inputs = setup_inputs


def setup_inputs(seed=0):
    import zlib

    import numpy as np

    out = dict(_drawn_inputs(seed))
    spreads = {}
    factors = {'cache_k': 8.0,
     'cache_v': 8.0,
     'state_gla_fwd': 8.0,
     'state_gla_bwd': 8.0,
     'q_norm': 8.0,
     'k_norm': 9.678,
     'gla_norm': 59.711,
     'ln1_g': 7.746,
     'ln1_b': 8.079,
     'router_group_b': 64.0,
     'router_expert_b': 64.0,
     'ln2_g': 7.449,
     'ln2_b': 8.016,
     'router_group_w': 3.969,
     'router_expert_w': 3.969,
     'exp_w_gate': 3.767,
     'exp_w_up': 3.447,
     'exp_w_down': 3.471}
    for name, (base, spread) in spreads.items():
        noise = np.random.default_rng([zlib.crc32(name.encode()), seed]).standard_normal(out[name].shape)
        drawn = base * np.exp(spread * noise) if base else spread * noise
        out[name] = __import__('jax').numpy.asarray(drawn.astype(out[name].dtype))
    for name, factor in factors.items():
        out[name] = (out[name] * factor).astype(out[name].dtype)
    return out
```

```python
import numpy as np
from contextlib import ExitStack

import concourse.bass as bass
from concourse import mybir

fp32 = mybir.dt.float32
u32 = mybir.dt.uint32
ALU = mybir.AluOpType
ACT = mybir.ActivationFunctionType
AX = mybir.AxisListType

P = 128
D = 1024
KT = D // P
N_LAT, N_CTX, N_PAST = 256, 128, 128
LAT_TILES, TILES = N_LAT // P, (N_LAT + N_CTX) // P
CTX = TILES - 1
TOKENS = TILES * P
HALF = 512
HEADS, KV, HD = 8, 2, 64
GH, DK, DV = 4, 64, 128
PAIRS = GH // 2
CHUNK = 64
RANK = 16
GROUPS, EPG, NE, DE = 4, 8, 32, 256
TOPK = 2
SLOT_ROWS = 64
ROUNDS = TOKENS // SLOT_ROWS
ALPHA = 2.0 ** 0.25
EPS = 1e-6
TAU = 16.0
BIG = 1.0e30
IN_WIDTHS = (HEADS * HD, KV * HD, KV * HD, GH * DK, GH * DK, GH * DV, GH * DV, 2 * RANK, 2 * D)
OFF = [0]
for _w in IN_WIDTHS:
    OFF.append(OFF[-1] + _w)
KVL = 2 * KV * HD + 2 * RANK

CONSTS = dict(ident=P, incl_f=P, incl_b=P, excl_f=P, excl_b=P, before=P, ones=P, sel=2 * P,
              chunks=2, selcol=2, ropeC=LAT_TILES * HD, ropeS=LAT_TILES * HD,
              iota=NE, iota_rows=P, ids=TOPK * TILES * 2, half=1, mhalf=8)
CAT = {}
_at = 0
for _n, _w in CONSTS.items():
    CAT[_n] = _at
    _at += _w
NCONST = _at


def constants():
    c = np.zeros((P, NCONST), np.float32)

    def put(name, a):
        a = np.asarray(a, np.float32).reshape(P, -1)
        c[:, CAT[name]:CAT[name] + a.shape[1]] = a

    s, t = np.arange(P)[:, None], np.arange(P)[None, :]
    same = (s // CHUNK) == (t // CHUNK)
    put("ident", s == t)
    put("incl_f", (same & (s <= t)) / TAU)
    put("incl_b", (same & (s >= t)) / TAU)
    put("excl_f", (same & (s > t)) / TAU)
    put("excl_b", (same & (s < t)) / TAU)
    put("before", s < t)
    put("ones", np.ones((P, P)))
    rows = np.arange(P)
    put("sel", np.concatenate([np.repeat((rows % 32 == j)[:, None], P, 1) for j in range(2)], 1))
    put("chunks", np.stack([rows // CHUNK == j for j in range(2)], 1) / TAU)
    put("selcol", np.stack([rows % 32 == j for j in range(2)], 1))
    q = HD // 4
    inv = 10000.0 ** (-np.arange(q, dtype=np.float32) / q)
    cos, sin = [], []
    for i in range(LAT_TILES):
        tok = i * P + rows
        for pos in (tok // 64, tok % 64):
            ang = pos[:, None].astype(np.float32) * inv[None, :].astype(np.float32)
            cos += [np.cos(ang), np.cos(ang)]
            sin += [-np.sin(ang), np.sin(ang)]
    put("ropeC", np.concatenate(cos, 1))
    put("ropeS", np.concatenate(sin, 1))
    put("iota", np.repeat(np.arange(NE)[None], P, 0))
    put("iota_rows", np.repeat((np.arange(P) % SLOT_ROWS)[None], P, 0))
    ids = np.zeros((P, TOPK, TILES, 2))
    for k in range(TOPK):
        for i in range(TILES):
            ids[:, k, i, 0] = k * TOKENS + i * P + rows + 1
            ids[:, k, i, 1] = i * P + rows + 1
    put("ids", ids)
    put("half", rows // SLOT_ROWS - 2.0)
    put("mhalf", np.full((P, 8), -0.5))
    return c


WEIGHTS = ([("ada", n) for n in range(4)]
           + [(x, 0) for x in ("kvl", "gqk", "vg", "q", "rg")] + [("mg", n) for n in range(4)]
           + [("br", n) for n in range(2)] + [("ada", n) for n in range(4, 10)]
           + [("wo", n) for n in range(2)] + [("ada", n) for n in (10, 11)])
PROJ = [(x, n, i) for x, n in WEIGHTS if x in ("kvl", "gqk", "vg", "q", "rg", "mg") for i in range(TILES)]
HEAD_JOBS = [(i, h) for i in (2, 0, 1) for h in range(HEADS)]
AFTER = {j: [] for j in range(len(PROJ))}
AFTER[3] += [("lr", 0), ("kprep", 0)]
AFTER[4] += [("z", 0), ("lr", 1), ("kprep", 1)]
AFTER[5] += [("z", 1), ("lr", 2), ("kprep", 2)]
AFTER[6] += [("z", 2), ("cum", 0)]
AFTER[7] += [("tr", 0), ("cum", 1)]
AFTER[8] += [("tr", 1), ("at", 0), ("cum", 2)]
AFTER[9] += [("intra", 0), ("tr", 2), ("at", 1)]
AFTER[10] += [("intra", 1), ("at", 2), ("qprep", 0)]
AFTER[11] += [("intra", 2), ("chainL", 0), ("chainC", 0), ("qprep", 1)]
AFTER[12] += [("kT", 0), ("kT", 1), ("chainL", 1), ("chainC", 1), ("qprep", 2)]
AFTER[13] += [("kT", 2), ("kT", 3), ("chainL", 2), ("qT", 2)]
AFTER[14] += [("chainL", 3), ("qT", 0), ("qT", 1), ("gout", 2)]
AFTER[15] += [("gout", 0)]
AFTER[16] += [("gout", 1)]
AFTER[17] += [("gT", 2)]
AFTER[18] += [("gT", 0)]
AFTER[19] += [("gT", 1)]
LAG = 2
for _m in range(len(HEAD_JOBS) // 2 + LAG):
    _j = min(15 + _m, len(PROJ) - 1)
    for _n in (2 * _m - 2, 2 * _m - 1):
        if 0 <= _n < len(HEAD_JOBS):
            AFTER[_j] += [("pT", _n)]
    for _n in (2 * _m, 2 * _m + 1):
        if _n < len(HEAD_JOBS):
            AFTER[_j] += [("score", _n)]
    for _n in (2 * _m - 4, 2 * _m - 3):
        if 0 <= _n < len(HEAD_JOBS):
            AFTER[_j] += [("pv", _n)]
            if _n % HEADS == HEADS - 1:
                AFTER[_j] += [("aout", HEAD_JOBS[_n][0])]
STEPS = [x for j in range(len(PROJ)) for x in AFTER[j]]


class Banks:

    def __init__(self, banks, full, read, jobs):
        self.at = {}
        uses = {b: 0 for b in range(len(banks))}
        for n, job in enumerate(jobs):
            b = n % len(banks)
            self.at[job] = (banks[b], full[b], read[b], uses[b])
            uses[b] += 1

    def bank(self, *job):
        return self.at[job][0]

    def claim(self, pe, *job):
        bank, _, read, k = self.at[job]
        if k:
            pe.wait_ge(read, k)
        return bank

    def filled(self, ins, *job):
        ins.then_inc(self.at[job][1], 1)

    def wait_full(self, eng, *job):
        bank, full, _, k = self.at[job]
        eng.wait_ge(full, k + 1)
        return bank

    def was_read(self, ins, *job):
        ins.then_inc(self.at[job][2], 1)

    def wait_read(self, eng, *job):
        eng.wait_ge(self.at[job][2], self.at[job][3] + 1)


def side_jobs():
    jobs = [("xT", 0, 0), ("xT", 0, 1), ("modc", 0)] + [("xT", i, g) for i in (1, 2) for g in range(2)]
    for kind, a in STEPS:
        if kind == "cum":
            jobs += [("cum", a), ("rest", a), ("decay", a)]
        elif kind == "tr":
            jobs += [("qgT", a), ("kgT", a)]
        elif kind == "at":
            jobs += [("at", a, 0), ("at", a, 1)]
        elif kind == "chainL":
            jobs += [("uL", a, d) for d in range(2) if a < 3]
        elif kind == "chainC":
            jobs += [("uC", a, d) for d in range(2)]
        elif kind in ("lr", "z", "kT", "qT", "gT", "pT", "score"):
            jobs += [(kind, a)]
    jobs += [("aT", i) for i in (2, 0, 1)]
    jobs += [("bc", n, s) for n in range(4, 10) for s in range(2)]
    jobs += [("mT", i, g) for i in range(TILES) for g in range(2)]
    jobs += [("hT", i, g) for i in range(TILES) for g in range(2)]
    jobs += [("router", i) for i in range(TILES)]
    jobs += [("bc", n, s) for n in (10, 11) for s in range(2)]
    jobs += [("rank", i) for i in range(TILES)] + [("count", 0)]
    return jobs


def main_jobs():
    jobs = [("ada", n) for n in range(4)] + [("proj",) + x for x in PROJ]
    jobs += [("br", n, i, m) for n in range(2) for i in range(TILES) for m in range(2)]
    jobs += [("ada", n) for n in range(4, 10)]
    jobs += [("wo", n, i) for i in range(TILES) for n in range(2)]
    jobs += [("ada", n) for n in (10, 11)]
    return jobs


def program(nc, T):
    ctx = ExitStack()
    with ctx:
        def sb(name, shape, dt=fp32):
            return ctx.enter_context(nc.sbuf_tensor(name, shape, dt))

        def sem(name):
            return ctx.enter_context(nc.semaphore(name))

        cst = sb("cst", [P, NCONST])

        def const(name, a=0, b=None):
            return cst[:, CAT[name] + a:CAT[name] + (CONSTS[name] if b is None else b)]

        ident = const("ident")
        qnorm = sb("qnorm", [P, HD])
        knorm = sb("knorm", [P, HD])
        gnorm = sb("gnorm", [P, DV])
        zbias = sb("zbias", [P, 2 * GH * DK])
        rbias = sb("rbias", [P, GROUPS + NE])
        wgate2 = sb("wgate2", [2 * RANK, 2 * GH * DK])
        wrouter = sb("wrouter", [P, KT, GROUPS + NE])
        cond = sb("cond", [P, 2, KT])
        conde = sb("conde", [P, 2, KT])
        csil = sb("csil", [P, KT, 32])
        PTr = sb("PTr", [P, 4, HALF])
        part = PTr
        abias = sb("abias", [P, 2, HALF])
        modc = sb("modc", [P, 2 * KT, 2])
        stats = sb("stats", [P, 2, 6])
        mv = sb("mv", [P, 2])
        rstd = sb("rstd", [P, 8])
        ss = sb("ss", [P, 8])
        lrT = sb("lrT", [2 * RANK, TOKENS])
        decay = sb("decay", [P, TILES, 8])
        negmax = sb("negmax", [P, 3])
        rowsum = sb("rowsum", [P, TILES, HEADS])
        rden = sb("rden", [P, HEADS])
        W = sb("W", [P, 2, KT * HALF])
        X = sb("X", [P, 24576])
        Y0 = sb("Y0", [P, TILES, KT, P])
        Y1 = sb("Y1", [P, TILES, 2, D])
        Y2 = sb("Y2", [P, TILES, D])

        at = [0]

        def carve(*shape):
            n = int(np.prod(shape))
            a = X[:, at[0]:at[0] + n]
            at[0] += n
            assert at[0] <= 24576
            names = [f"x{k}" for k in range(len(shape))]
            if len(shape) > 1:
                a = a.rearrange(f"p ({' '.join(names)}) -> p {' '.join(names)}",
                                **dict(zip(names[1:], shape[1:])))
            return a

        q = carve(TILES, HALF)
        kvl = carve(TILES, KVL)
        gqk = carve(TILES, 2, GH * DK)
        vg = carve(TILES, HALF)
        rg = carve(TILES, HALF)
        logg = carve(TILES, 2, GH * DK)
        E = carve(3, 2, GH * DK)
        qkt = carve(2, 2, GH * DK)
        kl = carve(TILES, 2, GH * DK)
        qgT = carve(TILES, 4, P)
        kgz = carve(4, 2, P)
        A = carve(2, GH, P)
        Sl = carve(2, PAIRS, 2 * DV)
        Sc = carve(2, PAIRS, 2 * DV)
        og = carve(HALF)
        tg = carve(HALF)
        qT = carve(TILES, 4, P)
        kTl = carve(KV, N_LAT + N_PAST)
        kTc = carve(KV, N_CTX)
        kc = carve(KV * HD)
        vc = carve(KV * HD)
        Pr = carve(4, 3 * P)
        hT = Y0
        x = Y2
        y2 = Y2[:, :, :].rearrange("p a b -> p (a b)")
        attnT = y2[:, 0:1536].rearrange("p (i k t) -> p i k t", i=TILES, k=4)
        glaT = y2[:, 1536:3072].rearrange("p (i k t) -> p i k t", i=TILES, k=4)
        t1 = glaT[:, 0, :, :].rearrange("p k t -> p (k t)")
        t2 = glaT[:, 1, :, :].rearrange("p k t -> p (k t)")
        mgs = Y1
        merged = lambda i: Y1[:, i, 0, :]
        x1 = lambda i: Y1[:, i, 1, :]
        mT = Y0
        h2T = Y0
        xr = lambda i: Y2[:, i, :]
        tail = X[:, 18432:24576].rearrange("p (a s d) -> p a s d", a=3, s=2)
        g1b, sc2b, sh2b = tail[:, 0], tail[:, 1], tail[:, 2]
        ln1 = lambda j: Y1[:, j, 0, :]
        SLOTW = 3 * KT * DE
        Wflat = W[:, :, :].rearrange("p a b -> p (a b)")
        eslot = [X[:, s * SLOTW:(s + 1) * SLOTW] for s in range(3)] + [Wflat[:, 0:SLOTW]]
        NSLOT = len(eslot)
        egu = [a[:, 0:2 * KT * DE].rearrange("p (g k n) -> p g k n", g=2, k=KT) for a in eslot]
        ed = [a[:, 2 * KT * DE:3 * KT * DE].rearrange("p (h n) -> p h n", h=2) for a in eslot]
        y0 = Y0[:, :, :, :].rearrange("p i k t -> p (i k t)")
        G = y0[:, 0:NSLOT * HALF].rearrange("p (b n) -> p b n", b=NSLOT)
        xTe = y0[:, NSLOT * HALF:(NSLOT + 2) * HALF].rearrange("p (b k n) -> p b k n", b=2, k=4)
        Yo = PTr
        g2b = Wflat[:, SLOTW:SLOTW + 2 * D].rearrange("p (s d) -> p s d", s=2)
        sg, hid, hidT = (abias[:, 0, k * P:(k + 1) * P] for k in range(3))
        fin = lambda i, k: (Y2, y0.rearrange("p (i n) -> p i n", i=TILES))[k][:, i, :]
        logit = sb("logit", [P, TILES, GROUPS + NE])
        gmask = sb("gmask", [P, TILES, GROUPS])
        gtmp = sb("gtmp", [P, TILES, GROUPS])
        lem = sb("lem", [P, TILES, NE])
        ltmp = sb("ltmp", [P, TILES, NE])
        oh = sb("oh", [P, TOPK, TILES, NE])
        both = sb("both", [P, TILES, NE])
        rv = sb("rv", [P, 8, TILES])
        wk = sb("wk", [P, TOPK, TILES])
        rk = sb("rk", [P, TOPK, TILES])
        cnt = sb("cnt", [P, NE])
        maxu = sb("maxu", [P, 1], u32)
        Rk = y2[:, 0:TOPK * TILES * P].rearrange("p (j n) -> p j n", n=P)
        idr = y2[:, 1024:1024 + TOPK * TILES * 2 * NE].rearrange("p (j c n) -> p j c n", c=2, n=NE)
        rank = sb("rank", [P, TILES, NE])
        tabs = sb("tabs", [P, 2, NE])
        tmpi = sb("tmpi", [P, 2, NE])
        gidx = sb("gidx", [P, NE + NSLOT], u32)
        sidx = sb("sidx", [P, NE], u32)
        gi = sb("gi", [P, NSLOT], u32)
        si = sb("si", [P, NSLOT], u32)
        zu = sb("zu", [P, 1], u32)

        h2_d = nc.dram_tensor("h2_rows", [TOKENS * 2, HALF], fp32).ap()
        yp_d = nc.dram_tensor("pair_rows", [TOPK * TOKENS * 2, HALF], fp32).ap()

        banks = [ctx.enter_context(nc.psum_tensor(f"bank{i}", [P, HALF], fp32)) for i in range(8)]
        full = [sem(f"bank{i}_full") for i in range(8)]
        read = [sem(f"bank{i}_read") for i in range(8)]
        main = Banks(banks[0:2], full[0:2], read[0:2], main_jobs())
        side = Banks([banks[i] for i in (2, 3, 7)], [full[i] for i in (2, 3, 7)],
                     [read[i] for i in (2, 3, 7)], side_jobs())
        outb = [banks[4], banks[5], banks[6]]

        S = {n: sem(n) for n in (
            "consts_in cond_in params_in states_in zeros_set cond_exp cond_silu x_normed pow_asked "
            "pow_done dve_step act_step kprepped qk_decayed at_masked intra_done gla_full gla_read "
            "negmax_ready q_ready pv_done gout_exp att_normed gated merged_ready mg_sig "
            "ln1_in x1_ready h2_ready h2_stored h2T_used exp_asked exp_done ln2_in both_ready rank_ready "
            "zeros_g lexp logg_ready onehot_ready tables_full idx_ready xTe_full xTe_ready gu_full silu_ready "
            "hid_ready hT_full hT_ready y_full y_ready moe_done ctx_out final_in "
            "out_ready out_done lgt_ready z_ready pad_set settled round_done").split()}
        x_in = [sem(f"x_in{i}") for i in range(TILES)]
        xr_in = [sem(f"xr_in{i}") for i in range(TILES)]
        fin_in = [sem(f"fin_in{i}") for i in range(TILES)]
        w_in = [sem(f"w_in{j}") for j in range(2)]
        w_free = [sem(f"w_free{j}") for j in range(2)]
        b_in = [sem(f"b_in{j}") for j in range(2)]
        ew_in = [sem(f"ew_in{j}") for j in range(NSLOT)]
        ew_free = [sem(f"ew_free{j}") for j in range(NSLOT)]
        g_in = [sem(f"g_in{j}") for j in range(NSLOT)]
        scattered = [sem(f"scattered{j}") for j in range(NSLOT)]
        gi_set = [sem(f"gi_set{j}") for j in range(NSLOT)]
        si_set = [sem(f"si_set{j}") for j in range(NSLOT)]
        WJ = {w: j for j, w in enumerate(WEIGHTS)}
        WCOUNT, _c = {}, [0, 0]
        for j, w in enumerate(WEIGHTS):
            _c[j % 2] += 32 if w[0] in ("kvl", "br") else 16
            WCOUNT[w] = _c[j % 2]

        def stream(i):
            return 0 if i < LAT_TILES else 1

        block = ctx.enter_context(nc.Block())

        def load_expert(eng, e, s):
            for g, name in enumerate(("exp_w_gate", "exp_w_up")):
                src = T[name][0].rearrange("e (h p c) n -> p e h c n", h=2, p=P)
                eng.dma_start(egu[s][:, g].rearrange("p (h c) n -> p h c n", h=2),
                              pick(src, e)).then_inc(ew_in[s], 16)
            src = T["exp_w_down"][0].rearrange("e (h p) n -> p e h n", p=P)
            eng.dma_start(ed[s], pick(src, e)).then_inc(ew_in[s], 16)

        def pick(src, e):
            a = src[:, e:e + 1] if isinstance(e, int) else src[:, bass.ds(e, 1)]
            names = "a b c d"[0:2 * (len(a.shape) - 2) - 1]
            return a.rearrange(f"p e {names} -> p (e {names.split()[0]}) {' '.join(names.split()[1:])}")

        TURNS = NE // NSLOT

        def first(r, it):
            return isinstance(r, int) and isinstance(it, int) and r == 0 and it == 0

        def settle(eng):
            eng.sem_inc(S["settled"], 1)

        def overflow(eng, again):
            eng.wait_ge(S["rank_ready"], 1)
            most = eng.value_load(maxu[0:1, 0:1], min_val=0, max_val=TOKENS)
            with eng.Fori(1, ROUNDS) as r:
                with eng.If(r * SLOT_ROWS < most):
                    again(r)

        @block.sync
        def _(sp):
            sp.dma_start(cst[:, :], T["consts"]).then_inc(S["consts_in"], 16)
            wi = T["w_in"][0].rearrange("(k p) n -> p k n", p=P)
            wa = T["w_ada"][0].rearrange("(p k) n -> p k n", k=KT)
            for j, (kind, n) in enumerate(WEIGHTS):
                buf = W[:, j % 2, :]
                if j >= 2:
                    sp.wait_ge(w_free[j % 2], j // 2)
                if kind == "ada":
                    w = buf.rearrange("p (k n) -> p k n", k=KT)
                    sp.dma_start(w, wa[:, :, n * HALF:(n + 1) * HALF]).then_inc(w_in[j % 2], 16)
                elif kind == "kvl":
                    w = buf[:, 0:KT * KVL].rearrange("p (k n) -> p k n", k=KT)
                    sp.dma_start(w[:, :, 0:2 * KV * HD], wi[:, :, OFF[1]:OFF[3]]).then_inc(w_in[j % 2], 16)
                    sp.dma_start(w[:, :, 2 * KV * HD:KVL], wi[:, :, OFF[7]:OFF[8]]).then_inc(w_in[j % 2], 16)
                elif kind in ("gqk", "vg", "q", "rg", "mg"):
                    c = {"gqk": OFF[3], "vg": OFF[5], "q": 0, "rg": OFF[6], "mg": OFF[8] + n * HALF}[kind]
                    w = buf.rearrange("p (k n) -> p k n", k=KT)
                    sp.dma_start(w, wi[:, :, c:c + HALF]).then_inc(w_in[j % 2], 16)
                elif kind == "br":
                    w = buf.rearrange("p (m k n) -> p m k n", m=2, k=4)
                    for m, src in enumerate((T["w_br_attn"], T["w_br_gla"])):
                        sp.dma_start(w[:, m], src[0].rearrange("(k p) n -> p k n", p=P)
                                     [:, :, n * HALF:(n + 1) * HALF]).then_inc(w_in[j % 2], 16)
                else:
                    w = buf.rearrange("p (k n) -> p k n", k=KT)
                    sp.dma_start(w, T["w_out"][0].rearrange("(k p) n -> p k n", p=P)
                                 [:, :, n * HALF:(n + 1) * HALF]).then_inc(w_in[j % 2], 16)
                if kind == "ada" and n == 0:
                    for i in range(TILES):
                        src = T["x_sample"][0, i * P:(i + 1) * P, :] if i < LAT_TILES else T["x_prompt"][0]
                        sp.dma_start(x[:, i, :], src).then_inc(x_in[i], 16)
                if kind == "br" and n == 1:
                    side.wait_read(sp, "aT", 1)
                    side.wait_read(sp, "gT", 1)
                    sp.wait_ge(S["ctx_out"], 16 * 6)
                    for s in range(3):
                        load_expert(sp, s, s)
            sp.wait_ge(w_free[(len(WEIGHTS) - 1) % 2], (len(WEIGHTS) + 1) // 2)
            sp.wait_ge(w_free[len(WEIGHTS) % 2], len(WEIGHTS) // 2)
            load_expert(sp, 3, 3)
            with sp.Fori(1, TURNS) as it:
                for s in range(NSLOT):
                    sp.wait_ge(ew_free[s], it)
                    load_expert(sp, it * NSLOT + s, s)

            def again(r):
                with sp.Fori(0, TURNS) as it:
                    for s in range(NSLOT):
                        sp.wait_ge(ew_free[s], r * (TURNS) + it)
                        load_expert(sp, it * NSLOT + s, s)

            overflow(sp, again)
            sp.wait_ge(S["moe_done"], 1)
            for i in range(TILES):
                for k in range(TOPK):
                    r0 = (k * TOKENS + i * P) * 2
                    sp.dma_start(fin(i, k), yp_d[r0:r0 + 2 * P, :].rearrange("(p h) n -> p (h n)", h=2))\
                        .then_inc(fin_in[i], 16)
            for i in range(TILES):
                sp.wait_ge(S["out_ready"], i + 1)
                dst = T["o_sample"][0, i * P:(i + 1) * P, :] if i < LAT_TILES else T["o_prompt"][0]
                sp.dma_start(dst, fin(i, 0)).then_inc(S["out_done"], 16)
            sp.wait_ge(S["out_done"], 16 * TILES)

        @block.gpsimd
        def _(pool):
            for a in (csil[:, :, :], abias[:, :, :], wgate2[:, :]):
                nc.gpsimd.memset(a, 0.0).then_inc(S["zeros_set"], 1)
            for a in (Sl, Sc, kgz, A, kTl, kTc):
                nc.gpsimd.memset(a, 0.0).then_inc(S["zeros_g"], 1)
            nc.gpsimd.memset(zu[:, :], 0).then_inc(S["zeros_g"], 1)
            pool.wait_ge(S["consts_in"], 16)
            asked = [0]

            def power(n):
                asked[0] += 1
                pool.wait_ge(S["pow_asked"], asked[0])
                nc.gpsimd.tensor_tensor(rstd[:, 0:n], ss[:, 0:n], const("mhalf", 0, n), ALU.pow)\
                    .then_inc(S["pow_done"], 1)

            nc.gpsimd.memset(gidx[:, NE:NE + NSLOT], 4096).then_inc(S["pad_set"], 1)
            for i in range(TILES):
                power(1)
            for kind, a in STEPS:
                if kind == "kprep":
                    power(KV)
                elif kind == "qprep":
                    power(HEADS)
                elif kind == "gout":
                    power(GH)
                elif kind == "at":
                    for d in range(2):
                        side.wait_read(pool, "at", a, d)
                        sgn = 1 if d == 0 else -1
                        nc.gpsimd.affine_select(out=A[:, d], in_=A[:, d], compare_op=ALU.is_ge, fill=0.0, base=0,
                                                pattern=[[0, GH], [sgn, P]], channel_multiplier=-sgn)\
                            .then_inc(S["at_masked"], 1)
                elif kind == "chainC" and a == 1:
                    side.wait_read(pool, "uC", 1, 0)
                    side.wait_read(pool, "uC", 1, 1)
                    for d, o in ((0, T["o_sf"]), (1, T["o_sb"])):
                        for hh in range(2):
                            pool.dma_start(o[0, 0].rearrange("(a b) d e -> b d a e", b=2)[hh],
                                           Sc[hh * DK:(hh + 1) * DK, d, :, hh * DV:(hh + 1) * DV])\
                                .then_inc(S["ctx_out"], 16)
                    pool.wait_ge(S["kprepped"], TILES)
                    pool.dma_start(T["o_k"][0, 0].rearrange("t k d -> t (k d)"), kvl[:, CTX, 0:KV * HD])\
                        .then_inc(S["ctx_out"], 16)
                    pool.dma_start(T["o_v"][0, 0].rearrange("t k d -> t (k d)"), kvl[:, CTX, KV * HD:2 * KV * HD])\
                        .then_inc(S["ctx_out"], 16)
            for i in range(TILES):
                power(1)
                power(1)
                pool.wait_ge(S["h2_ready"], i + 1)
                pool.dma_start(h2_d[i * 2 * P:(i + 1) * 2 * P, :].rearrange("(p h) n -> p (h n)", h=2), xr(i))\
                    .then_inc(S["h2_stored"], 16)
            pool.wait_ge(S["h2_stored"], 16 * TILES)

            def gather(s, e, turn):
                nc.gpsimd.tensor_tensor(gi[:, s:s + 1], gidx[:, e], zu[:, :], ALU.add).then_inc(gi_set[s], 1)
                pool.wait_ge(gi_set[s], turn + 1)
                settle(pool)
                pool.indirect_dma_start(G[:, s, :], None, h2_d,
                                        bass.IndirectOffsetOnAxis(ap=gi[:, s:s + 1], axis=0),
                                        bounds_check=2 * TOKENS - 1, oob_is_err=False).then_inc(g_in[s], 16)

            def experts(r):
                pool.wait_ge(S["pad_set"], 1)
                pool.wait_ge(S["idx_ready"], r + 1)
                settle(pool)
                for s in range(NSLOT):
                    gather(s, slice(s, s + 1), r * (TURNS + 1))

                def turns(it):
                    for s in range(NSLOT):
                        n = it * NSLOT + s
                        pool.wait_ge(S["xTe_full"], r * (NE + 1) + n + 1)
                        settle(pool)
                        gather(s, bass.ds(n + NSLOT, 1) , r * (TURNS + 1) + it + 1)
                        if not first(r, it):
                            pool.wait_ge(scattered[s], (r * TURNS + it) * 16)
                            settle(pool)
                        nc.gpsimd.tensor_tensor(si[:, s:s + 1], sidx[:, bass.ds(n, 1)], zu[:, :], ALU.add)\
                            .then_inc(si_set[s], 1)
                        pool.wait_ge(si_set[s], r * TURNS + it + 1)
                        settle(pool)
                        pool.wait_ge(S["y_ready"], r * NE + n + 2)
                        settle(pool)
                        pool.indirect_dma_start(yp_d, bass.IndirectOffsetOnAxis(ap=si[:, s:s + 1], axis=0),
                                                Yo[:, s, :], None,
                                                bounds_check=2 * TOPK * TOKENS - 1, oob_is_err=False)\
                            .then_inc(scattered[s], 16)

                if isinstance(r, int):
                    turns(0)
                    with pool.Fori(1, TURNS) as it:
                        turns(it)
                else:
                    with pool.Fori(0, TURNS) as it:
                        turns(it)
                for s in range(NSLOT):
                    pool.wait_ge(g_in[s], (r + 1) * (TURNS + 1) * 16)
                    settle(pool)
                    pool.wait_ge(scattered[s], (r + 1) * TURNS * 16)
                    settle(pool)
                pool.wait_ge(S["xTe_ready"], (r + 1) * (NE + 1))
                settle(pool)
                pool.sem_inc(S["round_done"], 1)

            experts(0)
            overflow(pool, experts)
            pool.sem_inc(S["moe_done"], 1)
            for i in range(TILES):
                power(1)

        @block.vector
        def _(dve):
            V = nc.vector
            steps = [0]
            told = {}

            def step(ins):
                steps[0] += 1
                ins.then_inc(S["dve_step"], 1)
                dve.wait_ge(S["dve_step"], steps[0])

            def tell(ins, name):
                told[name] = told.get(name, 0) + 1
                ins.then_inc(S[name], 1)
                dve.wait_ge(S[name], told[name])

            powers = [0]

            def power(out, in_, scale, shift):
                powers[0] += 1
                V.tensor_scalar(out, in_, scale, shift, ALU.mult, ALU.add).then_inc(S["pow_asked"], 1)
                dve.wait_ge(S["pow_done"], powers[0])

            def norm(src, dst):
                for g in range(2):
                    step(V.bn_stats(stats[:, g, :], src[:, g * HALF:(g + 1) * HALF]))
                step(V.bn_aggr(mv[:, :], stats[:, :, :].rearrange("p a b -> p (a b)")))
                power(ss[:, 0:1], mv[:, 1:2], 1.0, EPS)
                return V.tensor_scalar(dst, src, mv[:, 0:1], rstd[:, 0:1], ALU.subtract, ALU.mult)

            def per_head(src, h):
                return src.rearrange("p (h d) -> p h d", h=h)

            def rms(src, h, w, scale, shift, gain):
                n = h * w
                step(V.tensor_tensor(t1[:, 0:n], src, src, ALU.mult))
                step(V.tensor_reduce(ss[:, 0:h], per_head(t1[:, 0:n], h), AX.X, ALU.add))
                power(ss[:, 0:h], ss[:, 0:h], scale, shift)
                step(V.tensor_tensor(per_head(src, h), per_head(src, h),
                                     rstd[:, 0:h].unsqueeze(2).to_broadcast([P, h, w]), ALU.mult))
                return V.tensor_tensor(per_head(src, h), per_head(src, h),
                                       gain.unsqueeze(1).to_broadcast([P, h, w]), ALU.mult)

            def rope(src, h, i):
                n, w4 = h * HD, HD // 4
                C = const("ropeC", i * HD, (i + 1) * HD).unsqueeze(1).to_broadcast([P, h, HD])
                sn = const("ropeS", i * HD, (i + 1) * HD).rearrange("p (a b c) -> p a b c", a=2, b=2)
                step(V.tensor_tensor(per_head(t1[:, 0:n], h), per_head(src, h), C, ALU.mult))
                v = src.rearrange("p (h a b c) -> p h a b c", h=h, a=2, b=2)
                o = t2[:, 0:n].rearrange("p (h a b c) -> p h a b c", h=h, a=2, b=2)
                for b in range(2):
                    step(V.tensor_tensor(o[:, :, :, b, :], v[:, :, :, 1 - b, :],
                                         sn[:, :, b, :].unsqueeze(1).to_broadcast([P, h, 2, w4]), ALU.mult))
                step(V.tensor_tensor(t1[:, 0:n], t1[:, 0:n], t2[:, 0:n], ALU.add))

            def modulation(n, first):
                bank = main.wait_full(dve, "ada", n)
                dve.wait_ge(b_in[n % 2], 16 * (n // 2 + 1))
                if not first:
                    if n - 4 >= 4:
                        side.wait_full(dve, "bc", n - 4, 1)
                ins = V.tensor_tensor(part[:, n % 4, :], bank[:, :], abias[:, n % 2, :], ALU.add)
                main.was_read(ins, "ada", n)

            dve.wait_ge(S["cond_exp"], 1)
            step(V.tensor_scalar_add(conde[:, :, :], conde[:, :, :], 1.0))
            step(V.reciprocal(conde[:, :, :], conde[:, :, :]))
            dve.wait_ge(S["zeros_set"], 3)
            for s in range(2):
                ins = V.tensor_tensor(csil[:, :, s], cond[:, s, :], conde[:, s, :], ALU.mult)
                tell(ins, "cond_silu")
            modulation(0, True)
            for i in range(TILES):
                dve.wait_ge(x_in[i], 16)
                tell(norm(x[:, i, :], x[:, i, :]), "x_normed")
                modulation(i + 1, True)
            bank = side.wait_full(dve, "modc", 0)
            mc = bank[:, 0:4 * KT].rearrange("p (k s) -> p k s", s=2)
            step(V.tensor_copy(modc[:, 0:KT, :], mc[:, 0:KT, :]))
            ins = V.tensor_scalar_add(modc[:, KT:2 * KT, :], mc[:, KT:2 * KT, :], 1.0)
            side.was_read(ins, "modc", 0)
            side.wait_read(dve, "modc", 0)
            for i in range(TILES):
                bank = side.wait_full(dve, "xT", i, 1)
                for j in range(4):
                    k = 4 + j
                    ins = V.tensor_scalar(hT[:, i, k, :], bank[:, j * P:(j + 1) * P],
                                          modc[:, KT + k, stream(i):stream(i) + 1],
                                          modc[:, k, stream(i):stream(i) + 1], ALU.mult, ALU.add)
                side.was_read(ins, "xT", i, 1)
            dve.wait_ge(S["params_in"], 16 * 7)

            def block_rows(hh):
                return slice(hh * DK, (hh + 1) * DK)

            gla_order = {2: 0, 0: 1, 1: 2}
            for kind, a in STEPS:
                if kind == "kprep":
                    main.wait_read(dve, "proj", "kvl", 0, a)
                    k = kvl[:, a, 0:KV * HD]
                    ins = rms(k, KV, HD, 1.0 / HD, EPS, knorm[:, :])
                    if a < LAT_TILES:
                        step(ins)
                        rope(k, KV, a)
                        ins = V.tensor_copy(k, t1[:, 0:KV * HD])
                    tell(ins, "kprepped")
                elif kind == "qprep":
                    main.wait_read(dve, "proj", "q", 0, a)
                    step(rms(q[:, a, :], HEADS, HD, 1.0, HD * EPS, qnorm[:, :]))
                    if a < LAT_TILES:
                        rope(q[:, a, :], HEADS, a)
                    else:
                        step(V.tensor_copy(t1, q[:, a, :]))
                    tell(V.tensor_copy(q[:, a, :].rearrange("p (j k d) -> p k j d", k=KV, d=HD),
                                       t1.rearrange("p (k j d) -> p k j d", k=KV, d=HD)), "q_ready")
                elif kind == "z":
                    bank = side.wait_full(dve, "z", a)
                    z = logg[:, a].rearrange("p d n -> p (d n)")
                    ins = V.tensor_tensor(z, bank[:, :], zbias[:, :], ALU.add)
                    side.was_read(ins, "z", a)
                    side.wait_read(dve, "z", a)
                    zz = kl[:, a].rearrange("p d n -> p (d n)")
                    tell(V.scalar_tensor_tensor(zz, z, -1.0, z, ALU.mult, ALU.min), "z_ready")
                    step(V.tensor_scalar_min(z, z, 0.0))
                    dve.wait_ge(S["lexp"], 2 * a + 2)
                    tell(V.tensor_tensor(z, z, zz, ALU.subtract), "logg_ready")
                elif kind == "cum":
                    ex = [E[:, j] for j in range(3)]
                    side.wait_read(dve, "rest", a)
                    if a:
                        side.wait_full(dve, "kgT", a - 1)
                    qk = gqk[:, a]
                    wide = [qk[:, j, :].unsqueeze(1).to_broadcast([P, 2, GH * DK]) for j in range(2)]
                    V.scalar_tensor_tensor(qkt[:, 0], wide[0], DK ** -0.5, ex[0], ALU.mult, ALU.mult)
                    V.tensor_tensor(qkt[:, 1], wide[1], ex[1], ALU.mult)
                    tell(V.tensor_tensor(kl[:, a], wide[1], ex[2], ALU.mult), "qk_decayed")
                elif kind == "tr":
                    bank = side.wait_full(dve, "kgT", a)
                    if a:
                        side.wait_full(dve, "at", a - 1, 1)
                    b4 = bank[:, :].rearrange("p (j t) -> p j t", j=4)
                    for hh in range(2):
                        ins = V.tensor_copy(kgz[block_rows(hh), :, hh, :], b4[block_rows(hh)])
                    side.was_read(ins, "kgT", a)
                elif kind in ("chainL", "chainC"):
                    lat = kind == "chainL"
                    St = Sl if lat else Sc
                    if lat and a == 3:
                        continue
                    if lat and a == 0:
                        dve.wait_ge(S["states_in"], 16 * 4)
                    for d in range(2):
                        c = a if d == 0 else (3 if lat else 1) - a
                        tile, cc = (c // 2, c % 2) if lat else (CTX, c)
                        bank = side.wait_full(dve, "uL" if lat else "uC", a, d)
                        for pr in range(PAIRS):
                            for hh in range(2):
                                rows, cols = block_rows(hh), slice(hh * DV, (hh + 1) * DV)
                                u = bank[rows, pr * 2 * DV + hh * DV:pr * 2 * DV + (hh + 1) * DV]
                                st = St[rows, d, pr, cols]
                                if not lat and a == 0:
                                    ins = V.tensor_copy(st, u)
                                else:
                                    dc = decay[rows, tile, d * 4 + pr * 2 + cc:d * 4 + pr * 2 + cc + 1]
                                    ins = V.scalar_tensor_tensor(st, st, dc, u, ALU.mult, ALU.add)
                        side.was_read(ins, "uL" if lat else "uC", a, d)
                        side.wait_read(dve, "uL" if lat else "uC", a, d)
                elif kind == "kT":
                    bank = side.wait_full(dve, "kT", a)
                    for hh in range(2):
                        dst = kTc[block_rows(hh), hh, :] if a == 2 else \
                            kTl[block_rows(hh), hh, (2 if a == 3 else a) * P:(2 if a == 3 else a) * P + P]
                        ins = V.tensor_copy(dst, bank[block_rows(hh), 0:P])
                    side.was_read(ins, "kT", a)
                elif kind == "gout":
                    dve.wait_ge(S["gla_full"], 1 if a == 2 else 2)
                    tell(V.tensor_copy(og, outb[a][:, :]), "gla_read")
                    step(V.tensor_tensor(tg, og, og, ALU.mult))
                    step(V.tensor_reduce(ss[:, 0:GH], per_head(tg, GH), AX.X, ALU.add))
                    power(ss[:, 0:GH], ss[:, 0:GH], 1.0 / DV, EPS)
                    step(V.tensor_tensor(per_head(og, GH), per_head(og, GH),
                                         rstd[:, 0:GH].unsqueeze(2).to_broadcast([P, GH, DV]), ALU.mult))
                    step(V.tensor_tensor(per_head(og, GH), per_head(og, GH),
                                         gnorm[:, :].unsqueeze(1).to_broadcast([P, GH, DV]), ALU.mult))
                    dve.wait_ge(S["gout_exp"], gla_order[a] + 1)
                    ex = E[:, a].rearrange("p d n -> p (d n)")
                    step(V.tensor_scalar_add(ex, ex, 1.0))
                    step(V.reciprocal(ex, ex))
                    step(V.tensor_tensor(og, og, ex, ALU.mult))
                    tell(V.tensor_tensor(rg[:, a, :], rg[:, a, :], og, ALU.mult), "gated")
                elif kind == "score":
                    i, h = HEAD_JOBS[a]
                    w = 3 * P if i < LAT_TILES else P
                    bank = side.wait_full(dve, "score", a)
                    if a >= 3:
                        side.wait_read(dve, "score", a - 3)
                    V.tensor_reduce(negmax[:, a % 3:a % 3 + 1], bank[:, 0:w], AX.X, ALU.max, negate=True)\
                        .then_inc(S["negmax_ready"], 1)
                elif kind == "pT":
                    i, h = HEAD_JOBS[a]
                    w = 3 * P if i < LAT_TILES else P
                    bank = side.wait_full(dve, "pT", a)
                    if a >= 4:
                        dve.wait_ge(S["pv_done"], a - 3)
                    ins = V.tensor_copy(PTr[:, a % 4, 0:w], bank[:, 0:w])
                    side.was_read(ins, "pT", a)
                elif kind == "aout":
                    n = HEAD_JOBS.index((a, HEADS - 1))
                    dve.wait_ge(S["pv_done"], n + 1)
                    step(V.reciprocal(rden[:, :], rowsum[:, a, :]))
                    tell(V.tensor_tensor(per_head(q[:, a, :], HEADS), per_head(outb[a][:, :], HEADS),
                                         rden[:, :].unsqueeze(2).to_broadcast([P, HEADS, HD]), ALU.mult),
                         "att_normed")

            for n in range(2):
                for i in range(TILES):
                    gate = [mgs[:, i, m, n * HALF:(n + 1) * HALF] for m in range(2)]
                    if n == 0:
                        dve.wait_ge(S["mg_sig"], i + 1)
                    for m in range(2):
                        bank = main.wait_full(dve, "br", n, i, m)
                        ins = V.tensor_tensor(gate[m], bank[:, :], gate[m], ALU.mult)
                        main.was_read(ins, "br", n, i, m)
                        main.wait_read(dve, "br", n, i, m)
                    tell(V.tensor_tensor(gate[0], gate[0], gate[1], ALU.add), "merged_ready")
            for n in range(4, 10):
                modulation(n, False)
            for i in range(TILES):
                for n in range(2):
                    cols = slice(n * HALF, (n + 1) * HALF)
                    side.wait_read(dve, "bc", 4 + n, 1)
                    bank = main.wait_full(dve, "wo", n, i)
                    ins = V.tensor_tensor(x1(i)[:, cols], bank[:, :], g1b[:, stream(i), cols], ALU.mult)
                    main.was_read(ins, "wo", n, i)
                    main.wait_read(dve, "wo", n, i)
                dve.wait_ge(xr_in[i], 16)
                step(V.scalar_tensor_tensor(x1(i), xr(i), ALPHA, x1(i), ALU.mult, ALU.add))
                step(norm(x1(i), x1(i)))
                dve.wait_ge(S["ln1_in"], 32)
                step(V.tensor_tensor(x1(i), x1(i), ln1(0), ALU.mult))
                step(V.tensor_tensor(x1(i), x1(i), ln1(1), ALU.add))
                step(norm(x1(i), xr(i)))
                side.wait_read(dve, "bc", 9, 1)
                step(V.tensor_tensor(xr(i), xr(i), sc2b[:, stream(i), :], ALU.mult))
                tell(V.tensor_tensor(xr(i), xr(i), sh2b[:, stream(i), :], ALU.add), "h2_ready")
            for n in (10, 11):
                modulation(n, False)

            for i in range(TILES):
                bank = side.wait_full(dve, "router", i)
                ins = V.tensor_tensor(logit[:, i, :], bank[:, 0:GROUPS + NE], rbias[:, :], ALU.add)
                side.was_read(ins, "router", i)
            side.wait_read(dve, "router", TILES - 1)

            def wide(a, n):
                return a.unsqueeze(2).to_broadcast([P, TILES, n])

            def ramp(n):
                return const("iota", 0, n).unsqueeze(1).to_broadcast([P, TILES, n])

            def first_of(values, best, tmp, out, n):
                step(V.tensor_tensor(tmp, values, wide(best, n), ALU.is_equal))
                step(V.scalar_tensor_tensor(tmp, tmp, -64.0, ramp(n), ALU.mult, ALU.add))
                step(V.tensor_reduce(rv[:, 7, :], tmp, AX.X, ALU.min))
                step(V.tensor_tensor(out, tmp, wide(rv[:, 7, :], n), ALU.is_equal))

            lg = logit[:, :, 0:GROUPS]
            step(V.tensor_reduce(rv[:, 0, :], lg, AX.X, ALU.max))
            first_of(lg, rv[:, 0, :], gtmp[:, :, :], gmask[:, :, :], GROUPS)
            tell(V.tensor_tensor(gtmp[:, :, :], lg, wide(rv[:, 0, :], GROUPS), ALU.subtract), "exp_asked")
            step(V.tensor_copy(lem[:, :, :], logit[:, :, GROUPS:GROUPS + NE]))
            l12 = lem[:, :, :].rearrange("p i (g e) -> p (i g) e", g=GROUPS)
            g12 = gmask[:, :, :].rearrange("p i g -> p (i g)")
            step(V.tensor_tensor(l12, l12, g12.unsqueeze(2).to_broadcast([P, TILES * GROUPS, EPG]), ALU.mult))
            step(V.tensor_scalar(g12, g12, -1.0, BIG, ALU.add, ALU.mult))
            step(V.tensor_tensor(l12, l12, g12.unsqueeze(2).to_broadcast([P, TILES * GROUPS, EPG]), ALU.add))
            for k in range(TOPK):
                step(V.tensor_reduce(rv[:, 1 + k, :], lem[:, :, :], AX.X, ALU.max))
                first_of(lem[:, :, :], rv[:, 1 + k, :], ltmp[:, :, :], oh[:, k], NE)
                if k == 0:
                    step(V.scalar_tensor_tensor(lem[:, :, :], oh[:, 0], -2 * BIG, lem[:, :, :], ALU.mult, ALU.add))
            tell(V.tensor_tensor(both[:, :, :], oh[:, 0], oh[:, 1], ALU.add), "both_ready")
            tell(V.tensor_tensor(rv[:, 3, :], rv[:, 2, :], rv[:, 1, :], ALU.subtract), "exp_asked")
            dve.wait_ge(S["exp_done"], 2)
            step(V.tensor_reduce(rv[:, 4, :], gtmp[:, :, :], AX.X, ALU.add))
            step(V.tensor_scalar_add(rv[:, 5, :], rv[:, 3, :], 1.0))
            step(V.tensor_tensor(rv[:, 4, :], rv[:, 4, :], rv[:, 5, :], ALU.mult))
            step(V.reciprocal(wk[:, 0, :], rv[:, 4, :]))
            step(V.tensor_tensor(wk[:, 1, :], wk[:, 0, :], rv[:, 3, :], ALU.mult))
            for i in range(TILES):
                bank = side.wait_full(dve, "rank", i)
                side.was_read(V.tensor_copy(rank[:, i, :], bank[:, 0:NE]), "rank", i)
            side.wait_read(dve, "rank", TILES - 1)
            bank = side.wait_full(dve, "count", 0)
            step(V.tensor_reduce(cnt[:, 0:1], bank[:, 0:NE], AX.X, ALU.max))
            V.tensor_copy(maxu[:, :], cnt[:, 0:1]).then_inc(S["rank_ready"], 1)
            for k in range(TOPK):
                step(V.tensor_tensor(ltmp[:, :, :], oh[:, k], rank[:, :, :], ALU.mult))
                step(V.tensor_reduce(rk[:, k, :], ltmp[:, :, :], AX.X, ALU.add))
            ohj = oh[:, :, :, :].rearrange("p k i n -> p (k i) n")
            dve.wait_ge(S["h2_stored"], 16 * TILES)
            side.wait_full(dve, "hT", TILES - 1, 1)
            ids = const("ids").rearrange("p (j c) -> p j c", c=2)
            for c in range(2):
                step(V.tensor_tensor(idr[:, :, c, :], ohj,
                                     ids[:, :, c].unsqueeze(2).to_broadcast([P, TOPK * TILES, NE]), ALU.mult))
            rkj = rk[:, :, :].rearrange("p k i -> p (k i)")

            def tables(r):
                if not isinstance(r, int):
                    dve.wait_ge(S["round_done"], r)
                for j in range(TOPK * TILES):
                    ins = V.tensor_scalar(Rk[:, j, :], const("iota_rows"), rkj[:, j:j + 1], None, ALU.is_equal)
                ins.then_inc(S["onehot_ready"], 1)
                dve.wait_ge(S["tables_full"], r + 1)
                tb = banks[4][:, 0:2 * NE].rearrange("p (c n) -> p c n", c=2)
                V.tensor_copy(tabs[:, :, :], tb).then_inc(S["lgt_ready"], 1)
                dve.wait_ge(S["lgt_ready"], 5 * r + 1)
                V.tensor_scalar(tmpi[:, :, :], tabs[:, :, :], 2.0, const("half"), ALU.mult, ALU.add)\
                    .then_inc(S["lgt_ready"], 1)
                dve.wait_ge(S["lgt_ready"], 5 * r + 2)
                V.tensor_scalar(gidx[:, 0:NE], tmpi[:, 1, :], 0.0, None, ALU.max).then_inc(S["lgt_ready"], 1)
                V.tensor_scalar(tabs[:, 1, :], tabs[:, 0, :], 0.0, 4096.0, ALU.is_equal, ALU.mult)\
                    .then_inc(S["lgt_ready"], 1)
                dve.wait_ge(S["lgt_ready"], 5 * r + 4)
                V.tensor_tensor(sidx[:, :], tmpi[:, 0, :], tabs[:, 1, :], ALU.add).then_inc(S["idx_ready"], 1)
                V.tensor_scalar(rkj, rkj, -float(SLOT_ROWS), None, ALU.add).then_inc(S["lgt_ready"], 1)
                dve.wait_ge(S["lgt_ready"], 5 * r + 5)

            V.sem_inc(S["y_ready"], 1)

            def experts(r):
                tables(r)
                settle(dve)

                def turns(it):
                    for s in range(NSLOT):
                        n = r * NE + it * NSLOT + s
                        dve.wait_ge(S["silu_ready"], n + 1)
                        V.tensor_tensor(hid, sg, banks[5][:, P:2 * P], ALU.mult).then_inc(S["hid_ready"], 1)
                        dve.wait_ge(S["hT_full"], n + 1)
                        V.tensor_copy(hidT, banks[1][:, 0:P]).then_inc(S["hT_ready"], 1)
                        dve.wait_ge(S["y_full"], n + 1)
                        settle(dve)
                        if not first(r, it):
                            dve.wait_ge(scattered[s], (r * TURNS + it) * 16)
                        V.tensor_copy(Yo[:, s, :], banks[6][:, :]).then_inc(S["y_ready"], 1)

                if isinstance(r, int):
                    turns(0)
                    with dve.Fori(1, TURNS) as it:
                        turns(it)
                else:
                    with dve.Fori(0, TURNS) as it:
                        turns(it)

            experts(0)
            overflow(dve, experts)

            dve.wait_ge(S["ln2_in"], 32)
            side.wait_read(dve, "bc", 11, 1)
            for i in range(TILES):
                f = fin(i, 0)
                dve.wait_ge(fin_in[i], 32)
                step(V.tensor_scalar(f, f, wk[:, 0, i:i + 1], None, ALU.mult))
                step(V.scalar_tensor_tensor(f, fin(i, 1), wk[:, 1, i:i + 1], f, ALU.mult, ALU.add))
                step(V.tensor_tensor(f, f, g2b[:, stream(i), :], ALU.mult))
                step(V.scalar_tensor_tensor(f, x1(i), ALPHA, f, ALU.mult, ALU.add))
                step(norm(f, f))
                step(V.tensor_tensor(f, f, sc2b[:, 0, :], ALU.mult))
                tell(V.tensor_tensor(f, f, sc2b[:, 1, :], ALU.add), "out_ready")

        @block.scalar
        def _(act):
            A_ = nc.scalar.activation
            act.dma_start(cond[:, 0, :], T["c"][0].rearrange("(p k) -> p k", k=KT)).then_inc(S["cond_in"], 16)
            act.dma_start(cond[:, 1, :], T["c_ctx"].rearrange("(p k) -> p k", k=KT)).then_inc(S["cond_in"], 16)
            act.wait_ge(S["zeros_set"], 3)

            def bias_rows(n):
                act.dma_start(abias[0:2, n % 2, :],
                              T["b_ada"][0:1, n * HALF:(n + 1) * HALF].to_broadcast([2, HALF])).then_inc(b_in[n % 2], 16)

            bias_rows(0)
            bias_rows(1)
            for dst, src in ((qnorm, T["q_norm"]), (knorm, T["k_norm"]), (gnorm, T["gla_norm"]),
                             (zbias, T["gla_b_gate"].rearrange("a j n -> a (j n)"))):
                act.dma_start(dst[:, :], src.to_broadcast([P, dst.shape[1]])).then_inc(S["params_in"], 16)
            act.dma_start(rbias[:, 0:GROUPS], T["router_group_b"].to_broadcast([P, GROUPS])).then_inc(S["params_in"], 16)
            act.dma_start(rbias[:, GROUPS:GROUPS + NE], T["router_expert_b"].to_broadcast([P, NE]))\
                .then_inc(S["params_in"], 16)
            act.dma_start(wrouter[:, :, 0:GROUPS], T["router_group_w"][0].rearrange("(k p) n -> p k n", p=P))\
                .then_inc(S["params_in"], 16)
            act.dma_start(wrouter[:, :, GROUPS:GROUPS + NE], T["router_expert_w"][0].rearrange("(k p) n -> p k n", p=P))\
                .then_inc(S["act_step"], 16)
            for d in range(2):
                act.dma_start(wgate2[d * RANK:(d + 1) * RANK, d * GH * DK:(d + 1) * GH * DK], T["gla_w_gate"][0, d])\
                    .then_inc(S["act_step"], 16)
            act.dma_start(kc, T["cache_k"][0, 0].rearrange("t k d -> t (k d)")).then_inc(S["act_step"], 16)
            act.dma_start(vc, T["cache_v"][0, 0].rearrange("t k d -> t (k d)")).then_inc(S["act_step"], 16)
            act.wait_ge(S["zeros_g"], 7)
            for d, src in enumerate((T["state_gla_fwd"], T["state_gla_bwd"])):
                for hh in range(2):
                    act.dma_start(Sl[hh * DK:(hh + 1) * DK, d, :, hh * DV:(hh + 1) * DV],
                                  src[0, 0].rearrange("(a b) d e -> b d a e", b=2)[hh]).then_inc(S["states_in"], 16)
            act.wait_ge(S["cond_in"], 32)
            A_(conde[:, :, :], cond[:, :, :], ACT.Exp, scale=-1.0).then_inc(S["cond_exp"], 1)
            for n in (2, 3):
                main.wait_read(act, "ada", n - 2)
                bias_rows(n)
            side.wait_read(act, "modc", 0)
            for i in range(TILES):
                bank = side.wait_full(act, "xT", i, 0)
                for k in range(4):
                    ins = A_(hT[:, i, k, :], bank[:, k * P:(k + 1) * P], ACT.Identity,
                             scale=modc[:, KT + k, stream(i):stream(i) + 1],
                             bias=modc[:, k, stream(i):stream(i) + 1])
                side.was_read(ins, "xT", i, 0)
            exps = [0]
            for j, (kind, n, i) in enumerate(PROJ):
                bank = main.wait_full(act, "proj", kind, n, i)
                dst = {"kvl": lambda: kvl[:, i, :], "gqk": lambda: gqk[:, i].rearrange("p a b -> p (a b)"),
                       "vg": lambda: vg[:, i, :], "q": lambda: q[:, i, :], "rg": lambda: rg[:, i, :],
                       "mg": lambda: mgs[:, i, n // 2, (n % 2) * HALF:(n % 2 + 1) * HALF]}[kind]()
                main.was_read(A_(dst, bank[:, 0:dst.shape[1]], ACT.Copy), "proj", kind, n, i)
                for what, a in AFTER[j]:
                    if what == "lr":
                        bank = side.wait_full(act, "lr", a)
                        side.was_read(A_(lrT[:, a * P:(a + 1) * P], bank[0:2 * RANK, 0:P], ACT.Copy), "lr", a)
                    elif what == "z":
                        act.wait_ge(S["z_ready"], a + 1)
                        zz = kl[:, a].rearrange("p d n -> p (d n)")
                        A_(zz, zz, ACT.Exp).then_inc(S["lexp"], 1)
                        act.wait_ge(S["lexp"], 2 * a + 1)
                        A_(zz, zz, ACT.Ln, bias=1.0).then_inc(S["lexp"], 1)
                    elif what == "cum":
                        if a:
                            act.wait_ge(S["qk_decayed"], a)
                        bank = side.wait_full(act, "cum", a)
                        flat = [E[:, j2].rearrange("p d n -> p (d n)") for j2 in range(3)]
                        A_(flat[0], bank[:, :], ACT.Exp)
                        side.was_read(A_(flat[1], bank[:, :], ACT.Exp, scale=-1.0), "cum", a)
                        bank = side.wait_full(act, "rest", a)
                        side.was_read(A_(flat[2], bank[:, :], ACT.Exp), "rest", a)
                        bank = side.wait_full(act, "decay", a)
                        side.was_read(A_(decay[:, a, :], bank[:, 0:8], ACT.Exp), "decay", a)
                    elif what == "tr":
                        bank = side.wait_full(act, "qgT", a)
                        side.was_read(A_(qgT[:, a].rearrange("p j t -> p (j t)"), bank[:, :], ACT.Copy), "qgT", a)
                    elif what == "at":
                        if a:
                            act.wait_ge(S["intra_done"], a)
                        for d in range(2):
                            bank = side.wait_full(act, "at", a, d)
                            b4 = bank[:, :].rearrange("p (h t) -> p h t", h=GH)
                            for c in range(2):
                                rows = slice(c * CHUNK, (c + 1) * CHUNK)
                                ins = A_(A[rows, d, :, rows], b4[rows, :, rows], ACT.Copy)
                            side.was_read(ins, "at", a, d)
                    elif what == "qT":
                        bank = side.wait_full(act, "qT", a)
                        side.was_read(A_(qT[:, a].rearrange("p j t -> p (j t)"), bank[:, :], ACT.Copy), "qT", a)
                    elif what == "gout":
                        main.wait_read(act, "proj", "rg", 0, a)
                        act.wait_ge(S["qk_decayed"], TILES)
                        A_(E[:, a].rearrange("p d n -> p (d n)"), rg[:, a, :], ACT.Exp, scale=-1.0)\
                            .then_inc(S["gout_exp"], 1)
                    elif what == "gT":
                        bank = side.wait_full(act, "gT", a)
                        side.was_read(A_(glaT[:, a].rearrange("p k t -> p (k t)"), bank[:, :], ACT.Copy), "gT", a)
                    elif what == "score":
                        ti, h = HEAD_JOBS[a]
                        w = 3 * P if ti < LAT_TILES else P
                        act.wait_ge(S["negmax_ready"], a + 1)
                        if a >= 4:
                            side.wait_full(act, "pT", a - 4)
                        bank = side.bank("score", a)
                        ins = A_(Pr[:, a % 4, 0:w], bank[:, 0:w], ACT.Exp, bias=negmax[:, a % 3:a % 3 + 1],
                                 accum_out=rowsum[:, ti, h:h + 1])
                        side.was_read(ins, "score", a)
            for i in (2, 0, 1):
                bank = side.wait_full(act, "aT", i)
                side.was_read(A_(attnT[:, i].rearrange("p k t -> p (k t)"), bank[:, :], ACT.Copy), "aT", i)
            for i in range(TILES):
                main.wait_read(act, "proj", "mg", 3, i)
                m = mgs[:, i].rearrange("p m n -> p (m n)")
                A_(m, m, ACT.Sigmoid).then_inc(S["mg_sig"], 1)
            for n in (4, 5):
                bias_rows(n)
            main.wait_full(act, "br", 1, TILES - 1, 1)
            for i in range(TILES):
                src = T["x_sample"][0, i * P:(i + 1) * P, :] if i < LAT_TILES else T["x_prompt"][0]
                act.dma_start(xr(i), src).then_inc(xr_in[i], 16)
            for n in range(4, 10):
                for s in range(2):
                    bank = side.wait_full(act, "bc", n, s)
                    dst = {2: g1b, 3: sh2b, 4: sc2b}[n // 2][:, s, (n % 2) * HALF:(n % 2 + 1) * HALF]
                    side.was_read(A_(dst, bank[:, :], ACT.Identity, bias=1.0 if n // 2 == 4 else 0.0), "bc", n, s)
                main.wait_read(act, "ada", n)
                if n + 2 < 12:
                    bias_rows(n + 2)
            for i in range(TILES):
                for g in range(2):
                    bank = side.wait_full(act, "mT", i, g)
                    side.was_read(A_(mT[:, i, 4 * g:4 * g + 4, :].rearrange("p k t -> p (k t)"), bank[:, :], ACT.Copy),
                                  "mT", i, g)
                if i < 2:
                    act.dma_start(ln1(i), (T["ln1_g"], T["ln1_b"])[i].to_broadcast([P, D])).then_inc(S["ln1_in"], 16)
            for i in range(TILES):
                for g in range(2):
                    bank = side.wait_full(act, "hT", i, g)
                    side.was_read(A_(h2T[:, i, 4 * g:4 * g + 4, :].rearrange("p k t -> p (k t)"), bank[:, :], ACT.Copy),
                                  "hT", i, g)
            for j in range(2):
                act.dma_start(sc2b[:, j, :], (T["ln2_g"], T["ln2_b"])[j].to_broadcast([P, D])).then_inc(S["ln2_in"], 16)
            for n in (10, 11):
                for s in range(2):
                    bank = side.wait_full(act, "bc", n, s)
                    side.was_read(A_(g2b[:, s, (n % 2) * HALF:(n % 2 + 1) * HALF], bank[:, :], ACT.Copy), "bc", n, s)
            act.wait_ge(S["exp_asked"], 1)
            A_(gtmp[:, :, :], gtmp[:, :, :], ACT.Exp).then_inc(S["exp_done"], 1)
            act.wait_ge(S["exp_asked"], 2)
            A_(rv[:, 3, :], rv[:, 3, :], ACT.Exp).then_inc(S["exp_done"], 1)

            def tokens(b):
                A_(xTe[:, b].rearrange("p k n -> p (k n)"), banks[0][:, :], ACT.Copy).then_inc(S["xTe_ready"], 1)

            def experts(r):
                act.wait_ge(S["xTe_full"], r * (NE + 1) + 1)
                tokens(0)
                with act.Fori(0, TURNS) as it:
                    for s in range(NSLOT):
                        n = it * NSLOT + s
                        act.wait_ge(S["gu_full"], r * NE + n + 1)
                        A_(sg, banks[5][:, 0:P], ACT.Silu).then_inc(S["silu_ready"], 1)
                        act.wait_ge(S["xTe_full"], r * (NE + 1) + n + 2)
                        tokens((s + 1) % 2)

            experts(0)
            overflow(act, experts)

        @block.tensor
        def _(pe):
            mm, tp = nc.tensor.matmul, nc.tensor.transpose

            def weights(*w):
                j = WJ[w]
                pe.wait_ge(w_in[j % 2], WCOUNT[w])
                return W[:, j % 2, :]

            def used(ins, *w):
                ins.then_inc(w_free[WJ[w] % 2], 1)

            def modulation(n):
                w = weights("ada", n).rearrange("p (k n) -> p k n", k=KT)
                bank = main.claim(pe, "ada", n)
                for k in range(KT):
                    j = k % 4
                    ins = mm(bank[32 * j:32 * j + 32, :], csil[:, k, :], w[:, k, :], start=k < 4, stop=k >= 4,
                             skip_group_check=True)
                main.filled(ins, "ada", n)
                main.wait_full(pe, "ada", n)
                pe.nop().then_inc(w_free[WJ[("ada", n)] % 2], 1)

            def broadcast(n):
                main.wait_read(pe, "ada", n)
                for s in range(2):
                    bank = side.claim(pe, "bc", n, s)
                    side.filled(mm(bank[:, :], const("sel", s * P, (s + 1) * P), part[:, n % 4, :],
                                   start=True, stop=True), "bc", n, s)

            pe.wait_ge(S["consts_in"], 16)
            pe.wait_ge(S["cond_silu"], 2)
            for n in range(4):
                modulation(n)

            def x_transposes(i, g):
                if g == 0:
                    pe.wait_ge(S["x_normed"], i + 1)
                bank = side.claim(pe, "xT", i, g)
                for j in range(4):
                    k = 4 * g + j
                    ins = tp(bank[:, j * P:(j + 1) * P], x[:, i, k * P:(k + 1) * P], ident)
                side.filled(ins, "xT", i, g)

            x_transposes(0, 0)
            x_transposes(0, 1)
            bank = side.claim(pe, "modc", 0)
            for n in range(4):
                main.wait_read(pe, "ada", n)
                for j in range(4):
                    k = 4 * n + j
                    ins = mm(bank[:, 2 * k:2 * k + 2], part[:, n, j * P:(j + 1) * P], const("selcol"),
                             start=True, stop=True)
            side.filled(ins, "modc", 0)
            for i in (1, 2):
                for g in range(2):
                    x_transposes(i, g)

            def project(kind, n, i):
                w = weights(kind, n)
                cols = KVL if kind == "kvl" else HALF
                w = w[:, 0:KT * cols].rearrange("p (k n) -> p k n", k=KT)
                if kind == "kvl":
                    for g in range(2):
                        side.wait_read(pe, "xT", i, g)
                bank = main.claim(pe, "proj", kind, n, i)
                for k in range(KT):
                    ins = mm(bank[:, 0:cols], hT[:, i, k, :], w[:, k, :], start=k == 0, stop=k == KT - 1)
                main.filled(ins, "proj", kind, n, i)
                if i == TILES - 1:
                    main.wait_full(pe, "proj", kind, n, i)
                    used(pe.nop(), kind, n)

            def intra(a):
                pe.wait_ge(S["at_masked"], 2 * a + 2)
                if a == 0:
                    main.wait_read(pe, "proj", "vg", 0, TILES - 1)
                for d in range(2):
                    for h in range(GH):
                        ins = mm(outb[a][:, h * DV:(h + 1) * DV], A[:, d, h, :], vg[:, a, h * DV:(h + 1) * DV],
                                 start=d == 0 and h == 0, stop=False, skip_group_check=True)
                ins.then_inc(S["intra_done"], 1)

            def chain(lat, a):
                St, name = (Sl, "uL") if lat else (Sc, "uC")
                where = []
                for d in range(2):
                    c = a if d == 0 else (3 if lat else 1) - a
                    where.append((c // 2, c % 2) if lat else (CTX, c))
                if lat and a == 0:
                    pe.wait_ge(S["states_in"], 64)
                if a:
                    for d in range(2):
                        side.wait_read(pe, name, a - 1, d)
                if lat or a:
                    for d, (tile, c) in enumerate(where):
                        for pr in range(PAIRS):
                            rows = slice(c * CHUNK, (c + 1) * CHUNK)
                            ins = mm(outb[tile][rows, pr * 2 * DV:(pr + 1) * 2 * DV], qgT[:, tile, 2 * d + pr, rows],
                                     St[:, d, pr, :], start=False, stop=False, skip_group_check=True)
                    if (lat and a == 3) or not lat:
                        ins.then_inc(S["gla_full"], 1)
                if lat and a == 3:
                    return
                for d, (tile, c) in enumerate(where):
                    bank = side.claim(pe, name, a, d)
                    for pr in range(PAIRS):
                        rows = slice(c * CHUNK, (c + 1) * CHUNK)
                        ins = mm(bank[:, pr * 2 * DV:(pr + 1) * 2 * DV], kl[rows, tile, d, pr * P:(pr + 1) * P],
                                 vg[rows, tile, pr * 2 * DV:(pr + 1) * 2 * DV], start=True, stop=True)
                    side.filled(ins, name, a, d)

            def four(job, src):
                bank = side.claim(pe, *job)
                for j in range(4):
                    ins = tp(bank[:, j * P:(j + 1) * P], src(j), ident)
                side.filled(ins, *job)

            gla_order = {2: 1, 0: 2, 1: 3}
            for j, (kind, n, i) in enumerate(PROJ):
                project(kind, n, i)
                for what, a in AFTER[j]:
                    if what == "lr":
                        if a == 0:
                            pe.wait_ge(S["act_step"], 16 * 5)
                        main.wait_read(pe, "proj", "kvl", 0, a)
                        bank = side.claim(pe, "lr", a)
                        side.filled(tp(bank[0:2 * RANK, 0:P], kvl[:, a, 2 * KV * HD:KVL], ident), "lr", a)
                    elif what == "z":
                        side.wait_read(pe, "lr", a)
                        bank = side.claim(pe, "z", a)
                        side.filled(mm(bank[:, :], lrT[:, a * P:(a + 1) * P], wgate2[:, :], start=True, stop=True),
                                    "z", a)
                    elif what == "cum":
                        pe.wait_ge(S["logg_ready"], a + 1)
                        for job, m in (("cum", "incl"), ("rest", "excl")):
                            bank = side.claim(pe, job, a)
                            for d, x_ in enumerate("fb"):
                                ins = mm(bank[:, d * GH * DK:(d + 1) * GH * DK], const(f"{m}_{x_}"), logg[:, a, d, :],
                                         start=True, stop=True)
                            side.filled(ins, job, a)
                        bank = side.claim(pe, "decay", a)
                        for d in range(2):
                            for pr in range(PAIRS):
                                c = 4 * d + 2 * pr
                                ins = mm(bank[:, c:c + 2], logg[:, a, d, pr * P:(pr + 1) * P], const("chunks"),
                                         start=True, stop=True)
                        side.filled(ins, "decay", a)
                    elif what == "tr":
                        pe.wait_ge(S["qk_decayed"], a + 1)
                        for job, m in (("qgT", 0), ("kgT", 1)):
                            four((job, a), lambda jj: qkt[:, m, jj // 2, (jj % 2) * P:(jj % 2 + 1) * P])
                    elif what == "at":
                        side.wait_read(pe, "qgT", a)
                        side.wait_read(pe, "kgT", a)
                        for d in range(2):
                            bank = side.claim(pe, "at", a, d)
                            for h in range(GH):
                                jj = 2 * d + h // 2
                                ins = mm(bank[:, h * P:(h + 1) * P], kgz[:, jj, h % 2, :], qgT[:, a, jj, :],
                                         start=True, stop=True)
                            side.filled(ins, "at", a, d)
                    elif what == "intra":
                        intra(a)
                    elif what in ("chainL", "chainC"):
                        chain(what == "chainL", a)
                    elif what == "kT":
                        if a < TILES:
                            pe.wait_ge(S["kprepped"], a + 1)
                        bank = side.claim(pe, "kT", a)
                        side.filled(tp(bank[:, 0:P], kvl[:, a, 0:KV * HD] if a < TILES else kc, ident), "kT", a)
                    elif what == "qT":
                        pe.wait_ge(S["q_ready"], a + 1)
                        four(("qT", a), lambda jj: q[:, a, jj * P:(jj + 1) * P])
                    elif what == "gT":
                        pe.wait_ge(S["gated"], gla_order[a])
                        four(("gT", a), lambda jj: rg[:, a, jj * P:(jj + 1) * P])
                    elif what == "score":
                        ti, h = HEAD_JOBS[a]
                        if h == 0:
                            side.wait_read(pe, "qT", ti)
                            side.wait_read(pe, "kT", 2)
                            side.wait_read(pe, "kT", 3)
                        bank = side.claim(pe, "score", a)
                        keys = kTl[:, h // 4, :] if ti < LAT_TILES else kTc[:, h // 4, :]
                        side.filled(mm(bank[:, 0:keys.shape[1]], qT[:, ti, h % 4, :], keys, start=True, stop=True),
                                    "score", a)
                    elif what == "pT":
                        ti, h = HEAD_JOBS[a]
                        side.wait_read(pe, "score", a)
                        bank = side.claim(pe, "pT", a)
                        for c in range(3 if ti < LAT_TILES else 1):
                            ins = tp(bank[:, c * P:(c + 1) * P], Pr[:, a % 4, c * P:(c + 1) * P], ident)
                        side.filled(ins, "pT", a)
                    elif what == "pv":
                        ti, h = HEAD_JOBS[a]
                        side.wait_read(pe, "pT", a)
                        if h == 0:
                            pe.wait_ge(S["gla_read"], gla_order[ti])
                        vcols = slice(KV * HD + (h // 4) * HD, KV * HD + (h // 4 + 1) * HD)
                        vals = [kvl[:, 0, vcols], kvl[:, 1, vcols], vc[:, (h // 4) * HD:(h // 4 + 1) * HD]] \
                            if ti < LAT_TILES else [kvl[:, CTX, vcols]]
                        for c, v in enumerate(vals):
                            ins = mm(outb[ti][:, h * HD:(h + 1) * HD], PTr[:, a % 4, c * P:(c + 1) * P], v,
                                     start=c == 0, stop=c == len(vals) - 1)
                        ins.then_inc(S["pv_done"], 1)
            for m, i in enumerate((2, 0, 1)):
                pe.wait_ge(S["att_normed"], m + 1)
                four(("aT", i), lambda jj: q[:, i, jj * P:(jj + 1) * P])

            for n in range(2):
                w = weights("br", n).rearrange("p (m k n) -> p m k n", m=2, k=4)
                for i in range(TILES):
                    if n == 0:
                        side.wait_read(pe, "aT", i)
                        side.wait_read(pe, "gT", i)
                    for m, src in enumerate((attnT, glaT)):
                        bank = main.claim(pe, "br", n, i, m)
                        for k in range(4):
                            ins = mm(bank[:, :], src[:, i, k, :], w[:, m, k, :], start=k == 0, stop=k == 3)
                        main.filled(ins, "br", n, i, m)
                main.wait_full(pe, "br", n, TILES - 1, 1)
                used(pe.nop(), "br", n)
            for n in range(4, 10):
                modulation(n)
                if n > 4:
                    broadcast(n - 1)
            broadcast(9)
            for i in range(TILES):
                pe.wait_ge(S["merged_ready"], TILES + i + 1)
                for g in range(2):
                    four(("mT", i, g), lambda jj: merged(i)[:, (4 * g + jj) * P:(4 * g + jj + 1) * P])
            for i in range(TILES):
                for g in range(2):
                    side.wait_read(pe, "mT", i, g)
                for n in range(2):
                    w = weights("wo", n).rearrange("p (k n) -> p k n", k=KT)
                    bank = main.claim(pe, "wo", n, i)
                    for k in range(KT):
                        ins = mm(bank[:, :], mT[:, i, k, :], w[:, k, :], start=k == 0, stop=k == KT - 1)
                    main.filled(ins, "wo", n, i)
                    if i == TILES - 1:
                        main.wait_full(pe, "wo", n, i)
                        used(pe.nop(), "wo", n)

            def second_transposes(i):
                pe.wait_ge(S["h2_ready"], i + 1)
                for g in range(2):
                    four(("hT", i, g), lambda jj: xr(i)[:, (4 * g + jj) * P:(4 * g + jj + 1) * P])

            for i in range(TILES):
                second_transposes(i)
            for n in (10, 11):
                modulation(n)
            for i in range(TILES):
                for g in range(2):
                    side.wait_read(pe, "hT", i, g)
                bank = side.claim(pe, "router", i)
                for k in range(KT):
                    ins = mm(bank[:, 0:GROUPS + NE], h2T[:, i, k, :], wrouter[:, k, :], start=k == 0, stop=k == KT - 1)
                side.filled(ins, "router", i)
            broadcast(10)
            broadcast(11)
            pe.wait_ge(S["both_ready"], 1)
            for i in range(TILES):
                bank = side.claim(pe, "rank", i)
                for j in range(i):
                    mm(bank[:, 0:NE], const("ones"), both[:, j, :], start=j == 0, stop=False)
                side.filled(mm(bank[:, 0:NE], const("before"), both[:, i, :], start=i == 0, stop=True), "rank", i)
            bank = side.claim(pe, "count", 0)
            for i in range(TILES):
                ins = mm(bank[:, 0:NE], const("ones"), both[:, i, :], start=i == 0, stop=i == TILES - 1)
            side.filled(ins, "count", 0)
            main.wait_read(pe, "ada", 10)
            main.wait_read(pe, "ada", 11)

            def tokens(b):
                g = G[:, b, :].rearrange("p (q c) -> p q c", c=4)
                for c in range(4):
                    ins = tp(banks[0][:, c * P:(c + 1) * P], g[:, :, c], ident)
                ins.then_inc(S["xTe_full"], 1)

            def experts(r):
                pe.wait_ge(S["onehot_ready"], r + 1)
                for j in range(TOPK * TILES):
                    ins = mm(banks[4][:, 0:2 * NE], Rk[:, j, :], idr[:, j].rearrange("p c n -> p (c n)"),
                             start=j == 0, stop=j == TOPK * TILES - 1)
                ins.then_inc(S["tables_full"], 1)
                pe.wait_ge(g_in[0], (r * (TURNS + 1) + 1) * 16)
                tokens(0)
                with pe.Fori(0, TURNS) as it:
                    for s in range(NSLOT):
                        n = it * NSLOT + s
                        x_, wgu, wd = xTe[:, s % 2], egu[s], ed[s]
                        pe.wait_ge(ew_in[s], (r * (TURNS) + it + 1) * 48)
                        pe.wait_ge(S["xTe_ready"], r * (NE + 1) + n + 1)
                        for k in range(KT):
                            h, c = k // 4, k % 4
                            for hh in range(2):
                                ins = mm(banks[5][hh * 64:hh * 64 + 64, 0:2 * P], x_[:, c, h * 64:h * 64 + 64],
                                         wgu[:, :, k, hh * P:(hh + 1) * P], start=k == 0, stop=k == KT - 1,
                                         skip_group_check=True)
                        ins.then_inc(S["gu_full"], 1)
                        pe.wait_ge(g_in[(s + 1) % NSLOT], (r * (TURNS + 1) + it + 1 + (s + 1) // NSLOT) * 16)
                        tokens((s + 1) % NSLOT)
                        pe.wait_ge(S["hid_ready"], r * NE + n + 1)
                        tp(banks[1][:, 0:P], hid, ident).then_inc(S["hT_full"], 1)
                        pe.wait_ge(S["hT_ready"], r * NE + n + 1)
                        pe.wait_ge(S["y_ready"], r * NE + n + 1)
                        for hh in range(2):
                            for o in range(2):
                                ins = mm(banks[6][o * 64:o * 64 + 64, :], hidT[:, hh * 64:hh * 64 + 64],
                                         wd[:, hh, o * HALF:(o + 1) * HALF], start=hh == 0, stop=hh == 1,
                                         skip_group_check=True)
                        ins.then_inc(S["y_full"], 1)
                        pe.wait_ge(S["y_full"], r * NE + n + 1)
                        pe.nop().then_inc(ew_free[s], 1)

            experts(0)
            overflow(pe, experts)


_INS = ["x_prompt", "x_sample", "cache_k", "cache_v", "state_gla_fwd", "state_gla_bwd", "c", "c_ctx", "w_ada",
        "b_ada", "w_in", "q_norm", "k_norm", "gla_w_gate", "gla_b_gate", "gla_norm", "w_br_attn", "w_br_gla",
        "w_out", "ln1_g", "ln1_b", "router_group_w", "router_group_b", "router_expert_w", "router_expert_b",
        "exp_w_gate", "exp_w_up", "exp_w_down", "ln2_g", "ln2_b"]
_OUTS = [("o_prompt", (1, N_CTX, D)), ("o_sample", (1, N_LAT, D)), ("o_k", (1, 1, N_CTX, KV, HD)),
         ("o_v", (1, 1, N_CTX, KV, HD)), ("o_sf", (1, 1, GH, DK, DV)), ("o_sb", (1, 1, GH, DK, DV))]


def kernel(**inputs):
    import concourse.bacc as _bacc
    from concourse.bass_utils import run_bass_kernel_spmd as _run

    nc = _bacc.Bacc("TRN2", target_bir_lowering=False, num_devices=1)
    arrays = {n: np.ascontiguousarray(inputs[n]) for n in _INS}
    arrays["consts"] = constants()
    tensors = {n: nc.dram_tensor(n, a.shape, fp32, kind="ExternalInput").ap() for n, a in arrays.items()}
    for n, shape in _OUTS:
        tensors[n] = nc.dram_tensor(n, shape, fp32, kind="ExternalOutput").ap()
    program(nc, tensors)
    r = _run(nc, [arrays], core_ids=[0])
    return tuple(r.results[0][n] for n, _ in _OUTS)
```

```python
import numpy as np
from contextlib import ExitStack

import concourse.bass as bass
from concourse import mybir

fp32 = mybir.dt.float32
u32 = mybir.dt.uint32
ALU = mybir.AluOpType
ACT = mybir.ActivationFunctionType
AX = mybir.AxisListType

P = 128
D = 1024
KT = D // P
N_LAT, N_CTX, N_PAST = 256, 128, 128
LAT_TILES, TILES = N_LAT // P, (N_LAT + N_CTX) // P
CTX = TILES - 1
TOKENS = TILES * P
HALF = 512
HEADS, KV, HD = 8, 2, 64
GH, DK, DV = 4, 64, 128
PAIRS = GH // 2
CHUNK = 64
RANK = 16
GROUPS, EPG, NE, DE = 4, 8, 32, 256
TOPK = 2
SLOT_ROWS = 64
ROUNDS = TOKENS // SLOT_ROWS
ALPHA = 2.0 ** 0.25
EPS = 1e-6
TAU = 16.0
BIG = 1.0e30
IN_WIDTHS = (HEADS * HD, KV * HD, KV * HD, GH * DK, GH * DK, GH * DV, GH * DV, 2 * RANK, 2 * D)
OFF = [0]
for _w in IN_WIDTHS:
    OFF.append(OFF[-1] + _w)
KVL = 2 * KV * HD + 2 * RANK

CONSTS = dict(ident=P, incl_f=P, incl_b=P, excl_f=P, excl_b=P, before=P, ones=P,
              chunks=2, selcol=2, ropeC=LAT_TILES * HD, ropeS=LAT_TILES * HD,
              iota=NE, iota_rows=P, ids=TOPK * TILES * 2, half=1, mhalf=8)
CAT = {}
_at = 0
for _n, _w in CONSTS.items():
    CAT[_n] = _at
    _at += _w
NCONST = _at


def constants():
    c = np.zeros((P, NCONST), np.float32)

    def put(name, a):
        a = np.asarray(a, np.float32).reshape(P, -1)
        c[:, CAT[name]:CAT[name] + a.shape[1]] = a

    s, t = np.arange(P)[:, None], np.arange(P)[None, :]
    same = (s // CHUNK) == (t // CHUNK)
    put("ident", s == t)
    put("incl_f", (same & (s <= t)) / TAU)
    put("incl_b", (same & (s >= t)) / TAU)
    put("excl_f", (same & (s > t)) / TAU)
    put("excl_b", (same & (s < t)) / TAU)
    put("before", s < t)
    put("ones", np.ones((P, P)))
    rows = np.arange(P)
    put("chunks", np.stack([rows // CHUNK == j for j in range(2)], 1) / TAU)
    put("selcol", np.stack([rows % 32 == j for j in range(2)], 1))
    q = HD // 4
    inv = 10000.0 ** (-np.arange(q, dtype=np.float32) / q)
    cos, sin = [], []
    for i in range(LAT_TILES):
        tok = i * P + rows
        for pos in (tok // 64, tok % 64):
            ang = pos[:, None].astype(np.float32) * inv[None, :].astype(np.float32)
            cos += [np.cos(ang), np.cos(ang)]
            sin += [-np.sin(ang), np.sin(ang)]
    put("ropeC", np.concatenate(cos, 1))
    put("ropeS", np.concatenate(sin, 1))
    put("iota", np.repeat(np.arange(NE)[None], P, 0))
    put("iota_rows", np.repeat((np.arange(P) % SLOT_ROWS)[None], P, 0))
    ids = np.zeros((P, TOPK, TILES, 2))
    for k in range(TOPK):
        for i in range(TILES):
            ids[:, k, i, 0] = k * TOKENS + i * P + rows + 1
            ids[:, k, i, 1] = i * P + rows + 1
    put("ids", ids)
    put("half", rows // SLOT_ROWS - 2.0)
    put("mhalf", np.full((P, 8), -0.5))
    return c


WEIGHTS = ([("ada", n) for n in range(4)]
           + [(x, 0) for x in ("kvl", "gqk", "vg", "q", "rg")] + [("mg", n) for n in range(4)]
           + [("br", n) for n in range(2)] + [("wo", n) for n in range(2)])
PROJ = [(x, n, i) for x, n in WEIGHTS if x in ("kvl", "gqk", "vg", "q", "rg", "mg") for i in range(TILES)]
HEAD_JOBS = [(i, h) for i in (2, 0, 1) for h in range(HEADS)]
AFTER = {j: [] for j in range(len(PROJ))}
AFTER[3] += [("lr", 0), ("kprep", 0)]
AFTER[4] += [("z", 0), ("lr", 1), ("kprep", 1)]
AFTER[5] += [("z", 1), ("lr", 2), ("kprep", 2)]
AFTER[6] += [("kT", 0), ("kT", 1), ("z", 2), ("cum", 0)]
AFTER[7] += [("kT", 2), ("kT", 3), ("tr", 0), ("cum", 1)]
AFTER[8] += [("tr", 1), ("at", 0), ("cum", 2)]
AFTER[9] += [("intra", 0), ("tr", 2), ("at", 1)]
AFTER[10] += [("intra", 1), ("at", 2), ("qprep", 0)]
AFTER[11] += [("intra", 2), ("chainL", 0), ("chainC", 0), ("qprep", 1)]
AFTER[12] += [("chainL", 1), ("chainC", 1), ("qprep", 2)]
AFTER[13] += [("chainL", 2)]
AFTER[14] += [("chainL", 3), ("qT", 2), ("qT", 0), ("qT", 1), ("gout", 2)]
AFTER[16] += [("gT", 2)]
AFTER[17] += [("gout", 0)]
AFTER[19] += [("gT", 0)]
AFTER[20] += [("gout", 1)]
AFTER[22] += [("gT", 1)]
LAG = 2
for _m in range(len(HEAD_JOBS) // 2 + LAG):
    _j = min(15 + _m, len(PROJ) - 1)
    for _n in (2 * _m - 2, 2 * _m - 1):
        if 0 <= _n < len(HEAD_JOBS):
            AFTER[_j] += [("pT", _n)]
    for _n in (2 * _m, 2 * _m + 1):
        if _n < len(HEAD_JOBS):
            AFTER[_j] += [("score", _n)]
    for _n in (2 * _m - 4, 2 * _m - 3):
        if 0 <= _n < len(HEAD_JOBS):
            AFTER[_j] += [("pv", _n)]
            if _n % HEADS == HEADS - 1:
                AFTER[_j] += [("aout", HEAD_JOBS[_n][0])]
for _n, _j in zip(range(4, 12), (1, 3, 5, 7, 9, 11, 12, 14)):
    AFTER[_j + 1].insert(0, ("rows", _n))
    AFTER[_j].insert(0, ("ada", _n))
for _j, _i in ((14, 2), (17, 0), (20, 1)):
    AFTER[_j] += [("gout2", _i)]
    AFTER[_j + 1] += [("gout3", _i)]
STEPS = [x for j in range(len(PROJ)) for x in AFTER[j]]


class Banks:

    def __init__(self, banks, full, read, jobs):
        self.at = {}
        uses = {b: 0 for b in range(len(banks))}
        for n, job in enumerate(jobs):
            b = n % len(banks)
            self.at[job] = (banks[b], full[b], read[b], uses[b])
            uses[b] += 1

    def bank(self, *job):
        return self.at[job][0]

    def claim(self, pe, *job):
        bank, _, read, k = self.at[job]
        if k:
            pe.wait_ge(read, k)
        return bank

    def filled(self, ins, *job):
        ins.then_inc(self.at[job][1], 1)

    def wait_full(self, eng, *job):
        bank, full, _, k = self.at[job]
        eng.wait_ge(full, k + 1)
        return bank

    def was_read(self, ins, *job):
        ins.then_inc(self.at[job][2], 1)

    def wait_read(self, eng, *job):
        eng.wait_ge(self.at[job][2], self.at[job][3] + 1)


def side_jobs():
    jobs = [("modc", 0), ("xT", 0, 0), ("xT", 0, 1)] + [("xT", i, g) for i in (1, 2) for g in range(2)]
    for kind, a in STEPS:
        if kind == "cum":
            jobs += [("cum", a), ("rest", a), ("decay", a)]
        elif kind == "tr":
            jobs += [("qgT", a), ("kgT", a)]
        elif kind == "at":
            jobs += [("at", a, 0), ("at", a, 1)]
        elif kind == "chainL":
            jobs += [("uL", a, d) for d in range(2) if a < 3]
        elif kind == "chainC":
            jobs += [("uC", a, d) for d in range(2)]
        elif kind in ("lr", "z", "kT", "qT", "gT", "pT", "score", "rows"):
            jobs += [(kind, a)]
    jobs += [("aT", i) for i in (2, 0, 1)]
    jobs += [("mT", i, g) for i in range(TILES) for g in range(2)]
    jobs += [("hT", i, g) for i in range(TILES) for g in range(2)]
    jobs += [("rank",), ("count",)]
    return jobs


def main_jobs():
    jobs = [("ada", n) for n in range(4)]
    for j, x in enumerate(PROJ):
        jobs += [("proj",) + x] + [step for step in AFTER[j] if step[0] == "ada"]
    jobs += [("br", n, i, m) for n in range(2) for i in range(TILES) for m in range(2)]
    jobs += [("wo", n, i) for i in range(TILES) for n in range(2)] + [("router",)]
    return jobs


def program(nc, T):
    ctx = ExitStack()
    with ctx:
        def sb(name, shape, dt=fp32):
            return ctx.enter_context(nc.sbuf_tensor(name, shape, dt))

        def sem(name):
            return ctx.enter_context(nc.semaphore(name))

        cst = sb("cst", [P, NCONST])

        def const(name, a=0, b=None):
            return cst[:, CAT[name] + a:CAT[name] + (CONSTS[name] if b is None else b)]

        ident = const("ident")
        qnorm = sb("qnorm", [P, HD])
        knorm = sb("knorm", [P, HD])
        gnorm = sb("gnorm", [P, DV])
        zbias = sb("zbias", [P, 2 * GH * DK])
        rbias = sb("rbias", [P, GROUPS + NE])
        wgate2 = sb("wgate2", [P, 2 * GH * DK])
        wrouter = sb("wrouter", [P, KT, GROUPS + NE])
        cond = sb("cond", [P, 2, KT])
        conde = sb("conde", [P, 2, KT])
        csil = sb("csil", [P, KT, 32])
        PTr = sb("PTr", [P, 4, HALF])
        part = PTr
        abias = sb("abias", [P, 2, HALF])
        modc = sb("modc", [P, 2 * KT, 2])
        stats = sb("stats", [P, 2, 6])
        mv = sb("mv", [P, 2])
        rstd = sb("rstd", [P, 8])
        ss = sb("ss", [P, 8])
        lrT = sb("lrT", [2 * RANK, TOKENS])
        decay = sb("decay", [P, TILES, 8])
        negmax = sb("negmax", [P, 3])
        rowsum = sb("rowsum", [P, TILES, HEADS])
        rden = sb("rden", [P, HEADS])
        W = sb("W", [P, 2, KT * HALF])
        X = sb("X", [P, 24576])
        Y0 = sb("Y0", [P, TILES, KT, P])
        Y1 = sb("Y1", [P, TILES, 2, D])
        Y2 = sb("Y2", [P, TILES, D])

        at = [0]

        def carve(*shape):
            n = int(np.prod(shape))
            a = X[:, at[0]:at[0] + n]
            at[0] += n
            assert at[0] <= 24576
            names = [f"x{k}" for k in range(len(shape))]
            if len(shape) > 1:
                a = a.rearrange(f"p ({' '.join(names)}) -> p {' '.join(names)}",
                                **dict(zip(names[1:], shape[1:])))
            return a

        q = carve(TILES, HALF)
        kvl = carve(TILES, KVL)
        gqk = carve(TILES, 2, GH * DK)
        vg = carve(TILES, HALF)
        rg = carve(TILES, HALF)
        logg = carve(TILES, 2, GH * DK)
        E = carve(3, 2, GH * DK)
        qkt = carve(2, 2, GH * DK)
        kl = carve(TILES, 2, GH * DK)
        qgT = carve(TILES, 4, P)
        kgz = carve(4, 2, P)
        A = carve(2, GH, P)
        Sl = carve(2, PAIRS, 2 * DV)
        Sc = carve(2, PAIRS, 2 * DV)
        og = carve(HALF)
        tg = carve(HALF)
        qT = carve(TILES, 4, P)
        kTl = carve(KV, N_LAT + N_PAST)
        kTc = carve(KV, N_CTX)
        kc = carve(KV * HD)
        vc = carve(KV * HD)
        Pr = carve(4, 3 * P)
        hT = Y0
        x = Y2
        y2 = Y2[:, :, :].rearrange("p a b -> p (a b)")
        attnT = y2[:, 0:1536].rearrange("p (i k t) -> p i k t", i=TILES, k=4)
        glaT = y2[:, 1536:3072].rearrange("p (i k t) -> p i k t", i=TILES, k=4)
        t1 = glaT[:, 0, :, :].rearrange("p k t -> p (k t)")
        t2 = glaT[:, 1, :, :].rearrange("p k t -> p (k t)")
        mgs = Y1
        adabuf = Y1[:, :, :, :].rearrange("p i m n -> p (i m n)")[:, 0:KT * HALF]
        merged = lambda i: Y1[:, i, 0, :]
        x1 = lambda i: Y1[:, i, 1, :]
        mT = Y0
        h2T = Y0
        xr = lambda i: Y2[:, i, :]
        tail = X[:, 18432:24576].rearrange("p (a s d) -> p a s d", a=3, s=2)
        g1b, sc2b, sh2b = tail[:, 0], tail[:, 1], tail[:, 2]
        ln1 = lambda j: Y1[:, j, 0, :]
        ln2 = ln1
        SLOTW = 3 * KT * DE
        Wflat = W[:, :, :].rearrange("p a b -> p (a b)")
        eslot = [X[:, s * SLOTW:(s + 1) * SLOTW] for s in range(3)] + [Wflat[:, 0:SLOTW]]
        NSLOT = len(eslot)
        KD = KT * DE

        def views(gate, up, down0, down1):
            return ([a.rearrange("p (k n) -> p k n", k=KT) for a in (gate, up)], [down0, down1])

        ebuf = [views(a[:, 0:KD], a[:, KD:2 * KD], a[:, 2 * KD:2 * KD + D], a[:, 2 * KD + D:3 * KD]) for a in eslot]
        PARTED = NSLOT + 1
        OWN = {2: NSLOT, 3: PARTED}
        ebuf += [views(*(X[:, a:b] for a, b in ((3 * SLOTW, 3 * SLOTW + KD), (3 * SLOTW + KD, 3 * SLOTW + 2 * KD),
                                                (3 * SLOTW + 2 * KD, 3 * SLOTW + 2 * KD + D),
                                                (3 * SLOTW + 2 * KD + D, 4 * SLOTW)))),
                 views(Wflat[:, SLOTW:SLOTW + KD], y2[:, 0:KD], y2[:, KD:KD + D], merged(TILES - 1))]
        whole = eslot + [X[:, 3 * SLOTW:4 * SLOTW]]
        egu = [a[:, 0:2 * KD].rearrange("p (g k n) -> p g k n", g=2, k=KT) for a in whole]
        y0 = Y0[:, :, :, :].rearrange("p i k t -> p (i k t)")
        G = y0[:, 0:NSLOT * HALF].rearrange("p (b n) -> p b n", b=NSLOT)
        xTe = y0[:, NSLOT * HALF:(NSLOT + 2) * HALF].rearrange("p (b k n) -> p b k n", b=2, k=4)
        Yo = PTr
        g2b = X[:, 0:2 * D].rearrange("p (s d) -> p s d", s=2)
        sg, hid, hidT = (abias[:, 0, k * P:(k + 1) * P] for k in range(3))
        fin = lambda i, k: (Y2, y0.rearrange("p (i n) -> p i n", i=TILES))[k][:, i, :]
        logit = sb("logit", [P, TILES, GROUPS + NE])
        gmask = sb("gmask", [P, TILES, GROUPS])
        gtmp = sb("gtmp", [P, TILES, GROUPS])
        lem = sb("lem", [P, TILES, NE])
        ltmp = sb("ltmp", [P, TILES, NE])
        oh = sb("oh", [P, TOPK, TILES, NE])
        both = sb("both", [P, TILES, NE])
        rv = sb("rv", [P, 8, TILES])
        wk = sb("wk", [P, TOPK, TILES])
        rk = sb("rk", [P, TOPK, TILES])
        cnt = sb("cnt", [P, NE])
        maxu = sb("maxu", [P, 1], u32)
        Rk = [abias[:, 1, j * P:(j + 1) * P] for j in range(4)] + [zbias[:, j * P:(j + 1) * P] for j in range(2)]
        idr = wgate2[:, 0:TOPK * TILES * 2 * NE].rearrange("p (j c n) -> p j c n", c=2, n=NE)
        rank = sb("rank", [P, TILES, NE])
        tabs = sb("tabs", [P, 2, NE])
        tmpi = sb("tmpi", [P, 2, NE])
        gidx = sb("gidx", [P, NE + NSLOT], u32)
        sidx = sb("sidx", [P, NE], u32)
        gi = sb("gi", [P, NSLOT], u32)
        si = sb("si", [P, NSLOT], u32)
        zu = sb("zu", [P, 1], u32)

        h2_d = nc.dram_tensor("h2_rows", [TOKENS * 2, HALF], fp32).ap()
        mod_d = nc.dram_tensor("modulation_rows", [2, 8 * HALF], fp32).ap()
        yp_d = nc.dram_tensor("pair_rows", [TOPK * TOKENS * 2, HALF], fp32).ap()

        banks = [ctx.enter_context(nc.psum_tensor(f"bank{i}", [P, HALF], fp32)) for i in range(8)]
        full = [sem(f"bank{i}_full") for i in range(8)]
        read = [sem(f"bank{i}_read") for i in range(8)]
        main = Banks(banks[0:2], full[0:2], read[0:2], main_jobs())
        side = Banks([banks[i] for i in (2, 3, 7)], [full[i] for i in (2, 3, 7)],
                     [read[i] for i in (2, 3, 7)], side_jobs())
        outb = [banks[4], banks[5], banks[6]]

        S = {n: sem(n) for n in (
            "consts_in cond_in params_in states_in zeros_set cond_exp cond_silu x_normed pow_asked "
            "pow_done dve_step small_in kprepped qk_decayed at_masked intra_done gla_full gla_read "
            "negmax_ready q_ready pv_done gout_exp att_normed gated merged_ready mg_sig ln1_in h2_ready "
            "h2_stored exp_asked exp_done ln2_in both_ready rank_ready zeros_g lexp logg_ready "
            "onehot_ready tables_full idx_ready xTe_full xTe_ready gu_full silu_ready hid_ready hT_full "
            "hT_ready y_full y_ready moe_done ctx_out out_ready out_done table_step z_ready pad_set "
            "settled mod_stored mod_in gate2_in slots_done scaled paired gated2 round_done ada_in").split()}
        x_in = [sem(f"x_in{i}") for i in range(TILES)]
        xr_in = [sem(f"xr_in{i}") for i in range(TILES)]
        fin_in = [sem(f"fin_in{i}") for i in range(TILES)]
        w_in = [sem(f"w_in{j}") for j in range(2)]
        w_free = [sem(f"w_free{j}") for j in range(2)]
        b_in = [sem(f"b_in{j}") for j in range(2)]
        ew_in = [sem(f"ew_in{j}") for j in range(len(ebuf))]
        ed_in = [sem(f"ed_in{j}") for j in range(len(ebuf))]
        ew_free = [sem(f"ew_free{j}") for j in range(NSLOT)]
        g_in = [sem(f"g_in{j}") for j in range(NSLOT)]
        scattered = [sem(f"scattered{j}") for j in range(NSLOT)]
        gi_set = [sem(f"gi_set{j}") for j in range(NSLOT)]
        si_set = [sem(f"si_set{j}") for j in range(NSLOT)]
        WJ = {w: j for j, w in enumerate(WEIGHTS)}
        WCOUNT, _c = {}, [0, 0]
        for j, w in enumerate(WEIGHTS):
            _c[j % 2] += 32 if w[0] in ("kvl", "br") else 16
            WCOUNT[w] = _c[j % 2]

        def stream(i):
            return 0 if i < LAT_TILES else 1

        block = ctx.enter_context(nc.Block())

        def load_gate_up(eng, e, s):
            for g, name in enumerate(("exp_w_gate", "exp_w_up")):
                load_part(eng, name, g, e, s)

        def load_part(eng, name, g, e, s):
            src = T[name][0].rearrange("e (h p c) n -> p e h c n", h=2, p=P)
            eng.dma_start(ebuf[s][0][g].rearrange("p (h c) n -> p h c n", h=2), pick(src, e)).then_inc(ew_in[s], 16)

        def load_down(eng, e, s):
            if s == PARTED:
                for h in range(2):
                    eng.dma_start(ebuf[s][1][h], T["exp_w_down"][0, e, h * P:(h + 1) * P, :]).then_inc(ed_in[s], 16)
                return
            both_halves = whole[s][:, 2 * KD:3 * KD].rearrange("p (h n) -> p h n", h=2)
            src = T["exp_w_down"][0].rearrange("e (h p) n -> p e h n", p=P)
            eng.dma_start(both_halves, pick(src, e)).then_inc(ed_in[s], 16)

        def load_expert(eng, e, s):
            load_gate_up(eng, e, s)
            load_down(eng, e, s)

        def pick(src, e):
            a = src[:, e:e + 1] if isinstance(e, int) else src[:, bass.ds(e, 1)]
            names = "a b c d"[0:2 * (len(a.shape) - 2) - 1]
            return a.rearrange(f"p e {names} -> p (e {names.split()[0]}) {' '.join(names.split()[1:])}")

        TURNS = NE // NSLOT

        def first_expert(s):
            return s + NSLOT * (s in OWN)

        def slot_turns(s):
            return TURNS - (s in OWN)

        def first(r, it):
            return isinstance(r, int) and isinstance(it, int) and r == 0 and it == 0

        def settle(eng):
            eng.sem_inc(S["settled"], 1)

        def overflow(eng, again):
            eng.wait_ge(S["rank_ready"], 1)
            most = eng.value_load(maxu[0:1, 0:1], min_val=0, max_val=TOKENS)
            with eng.If(most > SLOT_ROWS):
                with eng.Fori(1, ROUNDS) as r:
                    with eng.If(r * SLOT_ROWS < most):
                        again(r)

        @block.sync
        def _(sp):
            sp.dma_start(cst[:, :], T["consts"]).then_inc(S["consts_in"], 16)

            def small_loads():
                sp.wait_ge(S["zeros_set"], 3)
                sp.wait_ge(S["zeros_g"], 7)
                for dst, src in ((qnorm, T["q_norm"]), (knorm, T["k_norm"]), (gnorm, T["gla_norm"]),
                                 (zbias, T["gla_b_gate"].rearrange("a j n -> a (j n)"))):
                    sp.dma_start(dst[:, :], src.to_broadcast([P, dst.shape[1]])).then_inc(S["params_in"], 16)
                sp.dma_start(rbias[:, 0:GROUPS], T["router_group_b"].to_broadcast([P, GROUPS])).then_inc(S["params_in"], 16)
                sp.dma_start(rbias[:, GROUPS:GROUPS + NE], T["router_expert_b"].to_broadcast([P, NE]))\
                    .then_inc(S["params_in"], 16)
                sp.dma_start(wrouter[:, :, 0:GROUPS], T["router_group_w"][0].rearrange("(k p) n -> p k n", p=P))\
                    .then_inc(S["params_in"], 16)
                sp.dma_start(wrouter[:, :, GROUPS:GROUPS + NE], T["router_expert_w"][0].rearrange("(k p) n -> p k n", p=P))\
                    .then_inc(S["small_in"], 16)
                for d in range(2):
                    sp.dma_start(wgate2[d * RANK:(d + 1) * RANK, d * GH * DK:(d + 1) * GH * DK], T["gla_w_gate"][0, d])\
                        .then_inc(S["small_in"], 16)
                sp.dma_start(kc, T["cache_k"][0, 0].rearrange("t k d -> t (k d)")).then_inc(S["small_in"], 16)
                sp.dma_start(vc, T["cache_v"][0, 0].rearrange("t k d -> t (k d)")).then_inc(S["small_in"], 16)
                for d, src in enumerate((T["state_gla_fwd"], T["state_gla_bwd"])):
                    for hh in range(2):
                        sp.dma_start(Sl[hh * DK:(hh + 1) * DK, d, :, hh * DV:(hh + 1) * DV],
                                      src[0, 0].rearrange("(a b) d e -> b d a e", b=2)[hh]).then_inc(S["states_in"], 16)

            wi = T["w_in"][0].rearrange("(k p) n -> p k n", p=P)
            wa = T["w_ada"][0].rearrange("(p k) n -> p k n", k=KT)
            for j, (kind, n) in enumerate(WEIGHTS):
                buf = W[:, j % 2, :]
                if j >= 2:
                    sp.wait_ge(w_free[j % 2], j // 2)
                if kind == "ada":
                    w = buf.rearrange("p (k n) -> p k n", k=KT)
                    sp.dma_start(w, wa[:, :, n * HALF:(n + 1) * HALF]).then_inc(w_in[j % 2], 16)
                elif kind == "kvl":
                    w = buf[:, 0:KT * KVL].rearrange("p (k n) -> p k n", k=KT)
                    sp.dma_start(w[:, :, 0:2 * KV * HD], wi[:, :, OFF[1]:OFF[3]]).then_inc(w_in[j % 2], 16)
                    sp.dma_start(w[:, :, 2 * KV * HD:KVL], wi[:, :, OFF[7]:OFF[8]]).then_inc(w_in[j % 2], 16)
                elif kind in ("gqk", "vg", "q", "rg", "mg"):
                    c = {"gqk": OFF[3], "vg": OFF[5], "q": 0, "rg": OFF[6], "mg": OFF[8] + n * HALF}[kind]
                    w = buf.rearrange("p (k n) -> p k n", k=KT)
                    sp.dma_start(w, wi[:, :, c:c + HALF]).then_inc(w_in[j % 2], 16)
                    if kind == "gqk":
                        small_loads()
                elif kind == "br":
                    w = buf.rearrange("p (m k n) -> p m k n", m=2, k=4)
                    for m, src in enumerate((T["w_br_attn"], T["w_br_gla"])):
                        sp.dma_start(w[:, m], src[0].rearrange("(k p) n -> p k n", p=P)
                                     [:, :, n * HALF:(n + 1) * HALF]).then_inc(w_in[j % 2], 16)
                else:
                    w = buf.rearrange("p (k n) -> p k n", k=KT)
                    sp.dma_start(w, T["w_out"][0].rearrange("(k p) n -> p k n", p=P)
                                 [:, :, n * HALF:(n + 1) * HALF]).then_inc(w_in[j % 2], 16)
                if kind == "ada" and n == 0:
                    for i in range(TILES):
                        src = T["x_sample"][0, i * P:(i + 1) * P, :] if i < LAT_TILES else T["x_prompt"][0]
                        sp.dma_start(x[:, i, :], src).then_inc(x_in[i], 16)
                if kind == "wo" and n == 1:
                    side.wait_read(sp, "aT", 1)
                    side.wait_read(sp, "gT", 1)
                    sp.wait_ge(S["ctx_out"], 16 * 6)
                    for s in range(3):
                        load_expert(sp, first_expert(s), s)
            sp.wait_ge(w_free[(len(WEIGHTS) - 1) % 2], (len(WEIGHTS) + 1) // 2)
            sp.wait_ge(w_free[len(WEIGHTS) % 2], len(WEIGHTS) // 2)
            load_expert(sp, first_expert(3), 3)
            load_part(sp, "exp_w_gate", 0, 3, PARTED)
            sp.wait_ge(S["h2_ready"], TILES)
            load_expert(sp, 2, OWN[2])
            sp.wait_ge(S["h2_stored"], 16 * TILES)
            side.wait_full(sp, "hT", TILES - 1, 1)
            load_part(sp, "exp_w_up", 1, 3, PARTED)
            load_down(sp, 3, PARTED)

            def reload(e, s, gu_done, down_done):
                sp.wait_ge(S["gu_full"], gu_done)
                load_gate_up(sp, e, s)
                sp.wait_ge(ew_free[s], down_done)
                load_down(sp, e, s)

            def round_loads(r):
                for s in range(NSLOT):
                    if s not in OWN:
                        reload(NSLOT + s, s, r * NE + s + 1, r * slot_turns(s) + 1)
                with sp.Fori(2, TURNS) as it:
                    for s in range(NSLOT):
                        reload(it * NSLOT + s, s, r * NE + (it - 1) * NSLOT + s + 1,
                               r * slot_turns(s) + it - (s in OWN))

            round_loads(0)

            def again(r):
                for s in range(NSLOT):
                    reload(first_expert(s), s, r * NE - NSLOT + s + 1, r * slot_turns(s))
                round_loads(r)

            overflow(sp, again)
            sp.wait_ge(S["slots_done"], 1)
            for st in range(2):
                sp.dma_start(g2b[:, st, :], mod_d[st:st + 1, 6 * HALF:8 * HALF].to_broadcast([P, D]))\
                    .then_inc(S["gate2_in"], 16)
            sp.wait_ge(S["moe_done"], 1)
            for i in range(TILES):
                for k in range(TOPK):
                    r0 = (k * TOKENS + i * P) * 2
                    sp.dma_start(fin(i, k), yp_d[r0:r0 + 2 * P, :].rearrange("(p h) n -> p (h n)", h=2))\
                        .then_inc(fin_in[i], 16)
            for i in range(TILES):
                sp.wait_ge(S["out_ready"], i + 1)
                dst = T["o_sample"][0, i * P:(i + 1) * P, :] if i < LAT_TILES else T["o_prompt"][0]
                sp.dma_start(dst, fin(i, 0)).then_inc(S["out_done"], 16)
            sp.wait_ge(S["out_done"], 16 * TILES)

        @block.gpsimd
        def _(pool):
            for a in (csil[:, :, :], abias[:, :, :], wgate2[0:2 * RANK, :]):
                nc.gpsimd.memset(a, 0.0).then_inc(S["zeros_set"], 1)
            for a in (Sl, Sc, kgz, A, kTl, kTc):
                nc.gpsimd.memset(a, 0.0).then_inc(S["zeros_g"], 1)
            nc.gpsimd.memset(zu[:, :], 0).then_inc(S["zeros_g"], 1)
            pool.wait_ge(S["consts_in"], 16)
            asked = [0]

            def power(n):
                asked[0] += 1
                pool.wait_ge(S["pow_asked"], asked[0])
                nc.gpsimd.tensor_tensor(rstd[:, 0:n], ss[:, 0:n], const("mhalf", 0, n), ALU.pow)\
                    .then_inc(S["pow_done"], 1)

            nc.gpsimd.memset(gidx[:, NE:NE + NSLOT], 4096).then_inc(S["pad_set"], 1)
            for i in range(TILES):
                power(1)
            for kind, a in STEPS:
                if kind == "kprep":
                    power(KV)
                elif kind == "qprep":
                    power(HEADS)
                elif kind == "gout":
                    power(GH)
                elif kind == "at":
                    for d in range(2):
                        side.wait_read(pool, "at", a, d)
                        sgn = 1 if d == 0 else -1
                        nc.gpsimd.affine_select(out=A[:, d], in_=A[:, d], compare_op=ALU.is_ge, fill=0.0, base=0,
                                                pattern=[[0, GH], [sgn, P]], channel_multiplier=-sgn)\
                            .then_inc(S["at_masked"], 1)
                elif kind == "chainC" and a == 1:
                    side.wait_read(pool, "uC", 1, 0)
                    side.wait_read(pool, "uC", 1, 1)
                    for d, o in ((0, T["o_sf"]), (1, T["o_sb"])):
                        for hh in range(2):
                            pool.dma_start(o[0, 0].rearrange("(a b) d e -> b d a e", b=2)[hh],
                                           Sc[hh * DK:(hh + 1) * DK, d, :, hh * DV:(hh + 1) * DV])\
                                .then_inc(S["ctx_out"], 16)
                    pool.wait_ge(S["kprepped"], TILES)
                    pool.dma_start(T["o_k"][0, 0].rearrange("t k d -> t (k d)"), kvl[:, CTX, 0:KV * HD])\
                        .then_inc(S["ctx_out"], 16)
                    pool.dma_start(T["o_v"][0, 0].rearrange("t k d -> t (k d)"), kvl[:, CTX, KV * HD:2 * KV * HD])\
                        .then_inc(S["ctx_out"], 16)
            for i in range(TILES):
                power(1)
                power(1)
                pool.wait_ge(S["h2_ready"], i + 1)
                pool.dma_start(h2_d[i * 2 * P:(i + 1) * 2 * P, :].rearrange("(p h) n -> p (h n)", h=2), xr(i))\
                    .then_inc(S["h2_stored"], 16)
            pool.wait_ge(S["h2_stored"], 16 * TILES)

            def gather(s, e, turn):
                nc.gpsimd.tensor_tensor(gi[:, s:s + 1], gidx[:, e], zu[:, :], ALU.add).then_inc(gi_set[s], 1)
                pool.wait_ge(gi_set[s], turn + 1)
                settle(pool)
                pool.indirect_dma_start(G[:, s, :], None, h2_d,
                                        bass.IndirectOffsetOnAxis(ap=gi[:, s:s + 1], axis=0),
                                        bounds_check=2 * TOKENS - 1, oob_is_err=False).then_inc(g_in[s], 16)

            def experts(r):
                pool.wait_ge(S["pad_set"], 1)
                pool.wait_ge(S["idx_ready"], r + 1)
                settle(pool)
                for s in range(NSLOT):
                    gather(s, slice(s, s + 1), r * (TURNS + 1))

                def turns(it):
                    for s in range(NSLOT):
                        n = it * NSLOT + s
                        pool.wait_ge(S["xTe_full"], r * (NE + 1) + n + 1)
                        settle(pool)
                        gather(s, bass.ds(n + NSLOT, 1) , r * (TURNS + 1) + it + 1)
                        if not first(r, it):
                            pool.wait_ge(scattered[s], (r * TURNS + it) * 16)
                            settle(pool)
                        nc.gpsimd.tensor_tensor(si[:, s:s + 1], sidx[:, bass.ds(n, 1)], zu[:, :], ALU.add)\
                            .then_inc(si_set[s], 1)
                        pool.wait_ge(si_set[s], r * TURNS + it + 1)
                        settle(pool)
                        pool.wait_ge(S["y_ready"], r * NE + n + 2)
                        settle(pool)
                        pool.indirect_dma_start(yp_d, bass.IndirectOffsetOnAxis(ap=si[:, s:s + 1], axis=0),
                                                Yo[:, s, :], None,
                                                bounds_check=2 * TOPK * TOKENS - 1, oob_is_err=False)\
                            .then_inc(scattered[s], 16)

                if isinstance(r, int):
                    turns(0)
                    with pool.Fori(1, TURNS) as it:
                        turns(it)
                else:
                    with pool.Fori(0, TURNS) as it:
                        turns(it)
                for s in range(NSLOT):
                    pool.wait_ge(g_in[s], (r + 1) * (TURNS + 1) * 16)
                    settle(pool)
                    pool.wait_ge(scattered[s], (r + 1) * TURNS * 16)
                    settle(pool)
                pool.wait_ge(S["xTe_ready"], (r + 1) * (NE + 1))
                settle(pool)
                pool.sem_inc(S["round_done"], 1)

            experts(0)
            overflow(pool, experts)
            pool.sem_inc(S["moe_done"], 1)
            pool.wait_ge(S["gate2_in"], 32)

            def gate(i):
                pool.wait_ge(S["paired"], i + 1)
                nc.gpsimd.tensor_tensor(fin(i, 0), fin(i, 0), g2b[:, stream(i), :], ALU.mult).then_inc(S["gated2"], 1)

            gate(0)
            gate(1)
            power(1)
            gate(2)
            power(1)
            power(1)

        @block.vector
        def _(dve):
            V = nc.vector
            steps = [0]
            told = {}

            def step(ins):
                steps[0] += 1
                ins.then_inc(S["dve_step"], 1)
                dve.wait_ge(S["dve_step"], steps[0])

            def tell(ins, name):
                told[name] = told.get(name, 0) + 1
                ins.then_inc(S[name], 1)
                dve.wait_ge(S[name], told[name])

            powers = [0]

            def ask_power(out, in_, scale, shift):
                powers[0] += 1
                V.tensor_scalar(out, in_, scale, shift, ALU.mult, ALU.add).then_inc(S["pow_asked"], 1)

            def power(out, in_, scale, shift):
                ask_power(out, in_, scale, shift)
                dve.wait_ge(S["pow_done"], powers[0])

            def norm(src, dst):
                for g in range(2):
                    step(V.bn_stats(stats[:, g, :], src[:, g * HALF:(g + 1) * HALF]))
                step(V.bn_aggr(mv[:, :], stats[:, :, :].rearrange("p a b -> p (a b)")))
                power(ss[:, 0:1], mv[:, 1:2], 1.0, EPS)
                return V.tensor_scalar(dst, src, mv[:, 0:1], rstd[:, 0:1], ALU.subtract, ALU.mult)

            def half_stats(src, g):
                return V.bn_stats(stats[:, g, :], src[:, g * HALF:(g + 1) * HALF])

            def norm_affine(src, dst, gain, shift, have_stats=False):
                if not have_stats:
                    half_stats(src, 0)
                    step(half_stats(src, 1))
                step(V.bn_aggr(mv[:, :], stats[:, :, :].rearrange("p a b -> p (a b)")))
                ask_power(ss[:, 0:1], mv[:, 1:2], 1.0, EPS)
                step(V.scalar_tensor_tensor(dst, src, mv[:, 0:1], gain, ALU.subtract, ALU.mult))
                dve.wait_ge(S["pow_done"], powers[0])
                return V.scalar_tensor_tensor(dst, dst, rstd[:, 0:1], shift, ALU.mult, ALU.add)

            def per_head(src, h):
                return src.rearrange("p (h d) -> p h d", h=h)

            def rms(src, h, w, scale, shift, gain):
                n = h * w
                step(V.tensor_tensor(t1[:, 0:n], src, src, ALU.mult))
                step(V.tensor_reduce(ss[:, 0:h], per_head(t1[:, 0:n], h), AX.X, ALU.add))
                power(ss[:, 0:h], ss[:, 0:h], scale, shift)
                step(V.tensor_tensor(per_head(src, h), per_head(src, h),
                                     rstd[:, 0:h].unsqueeze(2).to_broadcast([P, h, w]), ALU.mult))
                return V.tensor_tensor(per_head(src, h), per_head(src, h),
                                       gain.unsqueeze(1).to_broadcast([P, h, w]), ALU.mult)

            def rope(src, h, i):
                n, w4 = h * HD, HD // 4
                C = const("ropeC", i * HD, (i + 1) * HD).unsqueeze(1).to_broadcast([P, h, HD])
                sn = const("ropeS", i * HD, (i + 1) * HD).rearrange("p (a b c) -> p a b c", a=2, b=2)
                step(V.tensor_tensor(per_head(t1[:, 0:n], h), per_head(src, h), C, ALU.mult))
                v = src.rearrange("p (h a b c) -> p h a b c", h=h, a=2, b=2)
                o = t2[:, 0:n].rearrange("p (h a b c) -> p h a b c", h=h, a=2, b=2)
                for b in range(2):
                    step(V.tensor_tensor(o[:, :, :, b, :], v[:, :, :, 1 - b, :],
                                         sn[:, :, b, :].unsqueeze(1).to_broadcast([P, h, 2, w4]), ALU.mult))
                step(V.tensor_tensor(t1[:, 0:n], t1[:, 0:n], t2[:, 0:n], ALU.add))

            def modulation(n):
                bank = main.wait_full(dve, "ada", n)
                dve.wait_ge(b_in[n % 2], 16 * (n // 2 + 1))
                if n >= 8:
                    dve.wait_ge(S["mod_stored"], 16 * (n - 7))
                ins = V.tensor_tensor(part[:, n % 4, :], bank[:, :], abias[:, n % 2, :], ALU.add)
                main.was_read(ins, "ada", n)

            dve.wait_ge(S["cond_exp"], 1)
            step(V.tensor_scalar_add(conde[:, :, :], conde[:, :, :], 1.0))
            step(V.reciprocal(conde[:, :, :], conde[:, :, :]))
            dve.wait_ge(S["zeros_set"], 3)
            for s in range(2):
                ins = V.tensor_tensor(csil[:, :, s], cond[:, s, :], conde[:, s, :], ALU.mult)
                tell(ins, "cond_silu")
            modulation(0)
            for i in range(TILES):
                dve.wait_ge(x_in[i], 16)
                tell(norm(x[:, i, :], x[:, i, :]), "x_normed")
                modulation(i + 1)
            bank = side.wait_full(dve, "modc", 0)
            mc = bank[:, 0:4 * KT].rearrange("p (k s) -> p k s", s=2)
            step(V.tensor_copy(modc[:, 0:KT, :], mc[:, 0:KT, :]))
            ins = V.tensor_scalar_add(modc[:, KT:2 * KT, :], mc[:, KT:2 * KT, :], 1.0)
            side.was_read(ins, "modc", 0)
            side.wait_read(dve, "modc", 0)
            for i in range(TILES):
                bank = side.wait_full(dve, "xT", i, 1)
                for j in range(4):
                    k = 4 + j
                    ins = V.tensor_scalar(hT[:, i, k, :], bank[:, j * P:(j + 1) * P],
                                          modc[:, KT + k, stream(i):stream(i) + 1],
                                          modc[:, k, stream(i):stream(i) + 1], ALU.mult, ALU.add)
                side.was_read(ins, "xT", i, 1)
            dve.wait_ge(S["params_in"], 16 * 7)

            def block_rows(hh):
                return slice(hh * DK, (hh + 1) * DK)

            gla_order = {2: 0, 0: 1, 1: 2}
            for kind, a in STEPS:
                if kind == "ada":
                    modulation(a)
                elif kind == "rows":
                    bank = side.wait_full(dve, "rows", a)
                    side.was_read(V.tensor_scalar_add(part[0:2, a % 4, :], bank[0:2, :], float(a // 2 == 4)), "rows", a)
                elif kind == "kprep":
                    main.wait_read(dve, "proj", "kvl", 0, a)
                    k = kvl[:, a, 0:KV * HD]
                    ins = rms(k, KV, HD, 1.0 / HD, EPS, knorm[:, :])
                    if a < LAT_TILES:
                        step(ins)
                        rope(k, KV, a)
                        ins = V.tensor_copy(k, t1[:, 0:KV * HD])
                    tell(ins, "kprepped")
                elif kind == "qprep":
                    main.wait_read(dve, "proj", "q", 0, a)
                    step(rms(q[:, a, :], HEADS, HD, 1.0, HD * EPS, qnorm[:, :]))
                    if a < LAT_TILES:
                        rope(q[:, a, :], HEADS, a)
                    else:
                        step(V.tensor_copy(t1, q[:, a, :]))
                    tell(V.tensor_copy(q[:, a, :].rearrange("p (j k d) -> p k j d", k=KV, d=HD),
                                       t1.rearrange("p (k j d) -> p k j d", k=KV, d=HD)), "q_ready")
                elif kind == "z":
                    bank = side.wait_full(dve, "z", a)
                    z = logg[:, a].rearrange("p d n -> p (d n)")
                    ins = V.tensor_tensor(z, bank[:, :], zbias[:, :], ALU.add)
                    side.was_read(ins, "z", a)
                    side.wait_read(dve, "z", a)
                    zz = kl[:, a].rearrange("p d n -> p (d n)")
                    tell(V.scalar_tensor_tensor(zz, z, -1.0, z, ALU.mult, ALU.min), "z_ready")
                    step(V.tensor_scalar_min(z, z, 0.0))
                    dve.wait_ge(S["lexp"], 2 * a + 2)
                    tell(V.tensor_tensor(z, z, zz, ALU.subtract), "logg_ready")
                elif kind == "cum":
                    ex = [E[:, j] for j in range(3)]
                    side.wait_read(dve, "rest", a)
                    if a:
                        side.wait_full(dve, "kgT", a - 1)
                    qk = gqk[:, a]
                    wide = [qk[:, j, :].unsqueeze(1).to_broadcast([P, 2, GH * DK]) for j in range(2)]
                    V.scalar_tensor_tensor(qkt[:, 0], wide[0], DK ** -0.5, ex[0], ALU.mult, ALU.mult)
                    V.tensor_tensor(qkt[:, 1], wide[1], ex[1], ALU.mult)
                    tell(V.tensor_tensor(kl[:, a], wide[1], ex[2], ALU.mult), "qk_decayed")
                elif kind == "tr":
                    bank = side.wait_full(dve, "kgT", a)
                    if a:
                        side.wait_full(dve, "at", a - 1, 1)
                    b4 = bank[:, :].rearrange("p (j t) -> p j t", j=4)
                    for hh in range(2):
                        ins = V.tensor_copy(kgz[block_rows(hh), :, hh, :], b4[block_rows(hh)])
                    side.was_read(ins, "kgT", a)
                elif kind in ("chainL", "chainC"):
                    lat = kind == "chainL"
                    St = Sl if lat else Sc
                    if lat and a == 3:
                        continue
                    if lat and a == 0:
                        dve.wait_ge(S["states_in"], 16 * 4)
                    for d in range(2):
                        c = a if d == 0 else (3 if lat else 1) - a
                        tile, cc = (c // 2, c % 2) if lat else (CTX, c)
                        bank = side.wait_full(dve, "uL" if lat else "uC", a, d)
                        for pr in range(PAIRS):
                            for hh in range(2):
                                rows, cols = block_rows(hh), slice(hh * DV, (hh + 1) * DV)
                                u = bank[rows, pr * 2 * DV + hh * DV:pr * 2 * DV + (hh + 1) * DV]
                                st = St[rows, d, pr, cols]
                                if not lat and a == 0:
                                    ins = V.tensor_copy(st, u)
                                else:
                                    dc = decay[rows, tile, d * 4 + pr * 2 + cc:d * 4 + pr * 2 + cc + 1]
                                    ins = V.scalar_tensor_tensor(st, st, dc, u, ALU.mult, ALU.add)
                        side.was_read(ins, "uL" if lat else "uC", a, d)
                        side.wait_read(dve, "uL" if lat else "uC", a, d)
                elif kind == "kT":
                    bank = side.wait_full(dve, "kT", a)
                    for hh in range(2):
                        dst = kTc[block_rows(hh), hh, :] if a == 2 else \
                            kTl[block_rows(hh), hh, (2 if a == 3 else a) * P:(2 if a == 3 else a) * P + P]
                        ins = V.tensor_copy(dst, bank[block_rows(hh), 0:P])
                    side.was_read(ins, "kT", a)
                elif kind == "gout":
                    dve.wait_ge(S["gla_full"], 1 if a == 2 else 2)
                    tell(V.tensor_copy(og, outb[a][:, :]), "gla_read")
                    step(V.tensor_tensor(tg, og, og, ALU.mult))
                    step(V.tensor_reduce(ss[:, 0:GH], per_head(tg, GH), AX.X, ALU.add))
                    ask_power(ss[:, 0:GH], ss[:, 0:GH], 1.0 / DV, EPS)
                elif kind == "gout2":
                    dve.wait_ge(S["pow_done"], powers[0])
                    step(V.tensor_tensor(per_head(og, GH), per_head(og, GH),
                                         rstd[:, 0:GH].unsqueeze(2).to_broadcast([P, GH, DV]), ALU.mult))
                    step(V.tensor_tensor(per_head(og, GH), per_head(og, GH),
                                         gnorm[:, :].unsqueeze(1).to_broadcast([P, GH, DV]), ALU.mult))
                elif kind == "gout3":
                    dve.wait_ge(S["gout_exp"], gla_order[a] + 1)
                    ex = E[:, a].rearrange("p d n -> p (d n)")
                    step(V.tensor_scalar_add(ex, ex, 1.0))
                    step(V.reciprocal(ex, ex))
                    step(V.tensor_tensor(og, og, ex, ALU.mult))
                    tell(V.tensor_tensor(rg[:, a, :], rg[:, a, :], og, ALU.mult), "gated")
                elif kind == "score":
                    i, h = HEAD_JOBS[a]
                    w = 3 * P if i < LAT_TILES else P
                    bank = side.wait_full(dve, "score", a)
                    if a >= 3:
                        side.wait_read(dve, "score", a - 3)
                    V.tensor_reduce(negmax[:, a % 3:a % 3 + 1], bank[:, 0:w], AX.X, ALU.max, negate=True)\
                        .then_inc(S["negmax_ready"], 1)
                elif kind == "pT":
                    i, h = HEAD_JOBS[a]
                    w = 3 * P if i < LAT_TILES else P
                    bank = side.wait_full(dve, "pT", a)
                    if a >= 4:
                        dve.wait_ge(S["pv_done"], a - 3)
                    elif a == 0:
                        dve.wait_ge(S["mod_stored"], 16 * 8)
                    ins = V.tensor_copy(PTr[:, a % 4, 0:w], bank[:, 0:w])
                    side.was_read(ins, "pT", a)
                elif kind == "aout":
                    n = HEAD_JOBS.index((a, HEADS - 1))
                    dve.wait_ge(S["pv_done"], n + 1)
                    step(V.reciprocal(rden[:, :], rowsum[:, a, :]))
                    tell(V.tensor_tensor(per_head(q[:, a, :], HEADS), per_head(outb[a][:, :], HEADS),
                                         rden[:, :].unsqueeze(2).to_broadcast([P, HEADS, HD]), ALU.mult),
                         "att_normed")

            for n in range(2):
                for i in range(TILES):
                    gate = [mgs[:, i, m, n * HALF:(n + 1) * HALF] for m in range(2)]
                    if n == 0:
                        dve.wait_ge(S["mg_sig"], i + 1)
                    for m in range(2):
                        bank = main.wait_full(dve, "br", n, i, m)
                        ins = V.tensor_tensor(gate[m], bank[:, :], gate[m], ALU.mult)
                        main.was_read(ins, "br", n, i, m)
                        main.wait_read(dve, "br", n, i, m)
                    tell(V.tensor_tensor(gate[0], gate[0], gate[1], ALU.add), "merged_ready")
            for i in range(TILES):
                for n in range(2):
                    cols = slice(n * HALF, (n + 1) * HALF)
                    dve.wait_ge(S["mod_in"], 16 * 6)
                    bank = main.wait_full(dve, "wo", n, i)
                    ins = V.tensor_tensor(x1(i)[:, cols], bank[:, :], g1b[:, stream(i), cols], ALU.mult)
                    main.was_read(ins, "wo", n, i)
                    main.wait_read(dve, "wo", n, i)
                    dve.wait_ge(xr_in[i], 16)
                    step(V.scalar_tensor_tensor(x1(i)[:, cols], xr(i)[:, cols], ALPHA, x1(i)[:, cols],
                                                ALU.mult, ALU.add))
                    step(half_stats(x1(i), n))
                dve.wait_ge(S["ln1_in"], 32)
                step(norm_affine(x1(i), x1(i), ln1(0), ln1(1), have_stats=True))
                tell(norm_affine(x1(i), xr(i), sc2b[:, stream(i), :], sh2b[:, stream(i), :]), "h2_ready")

            bank = main.wait_full(dve, "router")
            ins = V.tensor_tensor(logit[:, :, :],
                                  bank[:, 0:TILES * (GROUPS + NE)].rearrange("p (i n) -> p i n", i=TILES),
                                  rbias[:, :].unsqueeze(1).to_broadcast([P, TILES, GROUPS + NE]), ALU.add)
            main.was_read(ins, "router")
            main.wait_read(dve, "router")

            def wide(a, n):
                return a.unsqueeze(2).to_broadcast([P, TILES, n])

            def ramp(n):
                return const("iota", 0, n).unsqueeze(1).to_broadcast([P, TILES, n])

            def first_of(values, best, tmp, out, n):
                step(V.tensor_tensor(tmp, values, wide(best, n), ALU.is_equal))
                step(V.scalar_tensor_tensor(tmp, tmp, -64.0, ramp(n), ALU.mult, ALU.add))
                step(V.tensor_reduce(rv[:, 7, :], tmp, AX.X, ALU.min))
                step(V.tensor_tensor(out, tmp, wide(rv[:, 7, :], n), ALU.is_equal))

            lg = logit[:, :, 0:GROUPS]
            step(V.tensor_reduce(rv[:, 0, :], lg, AX.X, ALU.max))
            first_of(lg, rv[:, 0, :], gtmp[:, :, :], gmask[:, :, :], GROUPS)
            l12 = lem[:, :, :].rearrange("p i (g e) -> p i g e", g=GROUPS)
            step(V.tensor_scalar(gmask[:, :, :], gmask[:, :, :], -1.0, BIG, ALU.add, ALU.mult))
            step(V.tensor_tensor(l12, logit[:, :, GROUPS:GROUPS + NE].rearrange("p i (g e) -> p i g e", g=GROUPS),
                                 gmask[:, :, :].unsqueeze(3).to_broadcast([P, TILES, GROUPS, EPG]), ALU.add))
            for k in range(TOPK):
                step(V.tensor_reduce(rv[:, 1 + k, :], lem[:, :, :], AX.X, ALU.max))
                first_of(lem[:, :, :], rv[:, 1 + k, :], ltmp[:, :, :], oh[:, k], NE)
                if k == 0:
                    step(V.scalar_tensor_tensor(lem[:, :, :], oh[:, 0], -2 * BIG, lem[:, :, :], ALU.mult, ALU.add))
            tell(V.tensor_tensor(both[:, :, :], oh[:, 0], oh[:, 1], ALU.add), "both_ready")
            tell(V.tensor_tensor(gtmp[:, :, :], lg, wide(rv[:, 0, :], GROUPS), ALU.subtract), "exp_asked")
            tell(V.tensor_tensor(rv[:, 3, :], rv[:, 2, :], rv[:, 1, :], ALU.subtract), "exp_asked")
            ohj = oh[:, :, :, :].rearrange("p k i n -> p (k i) n")
            ids = const("ids").rearrange("p (j c) -> p j c", c=2)
            for c in range(2):
                step(V.tensor_tensor(idr[:, :, c, :], ohj,
                                     ids[:, :, c].unsqueeze(2).to_broadcast([P, TOPK * TILES, NE]), ALU.mult))
            bank = side.wait_full(dve, "rank")
            for k in range(TOPK):
                ins = V.tensor_tensor(ltmp[:, :, :], oh[:, k],
                                      bank[:, 0:TILES * NE].rearrange("p (i n) -> p i n", i=TILES), ALU.mult)
                if k == 0:
                    step(ins)
                else:
                    side.was_read(ins, "rank")
                    side.wait_read(dve, "rank")
                step(V.tensor_reduce(rk[:, k, :], ltmp[:, :, :], AX.X, ALU.add))
            rkj = rk[:, :, :].rearrange("p k i -> p (k i)")

            def tables(r):
                if not isinstance(r, int):
                    dve.wait_ge(S["round_done"], r)
                for j in range(TOPK * TILES):
                    ins = V.tensor_scalar(Rk[j], const("iota_rows"), rkj[:, j:j + 1], None, ALU.is_equal)
                ins.then_inc(S["onehot_ready"], 1)
                dve.wait_ge(S["tables_full"], r + 1)
                tb = banks[4][:, 0:2 * NE].rearrange("p (c n) -> p c n", c=2)
                V.tensor_copy(tabs[:, :, :], tb).then_inc(S["table_step"], 1)
                dve.wait_ge(S["table_step"], 5 * r + 1)
                V.tensor_scalar(tmpi[:, :, :], tabs[:, :, :], 2.0, const("half"), ALU.mult, ALU.add)\
                    .then_inc(S["table_step"], 1)
                dve.wait_ge(S["table_step"], 5 * r + 2)
                V.tensor_scalar(tabs[:, 1, :], tabs[:, 0, :], 0.0, 4096.0, ALU.is_equal, ALU.mult)\
                    .then_inc(S["table_step"], 1)
                dve.wait_ge(S["table_step"], 5 * r + 3)
                V.tensor_tensor(gidx[:, 0:NE], tmpi[:, 1, :], tabs[:, 1, :], ALU.add).then_inc(S["table_step"], 1)
                dve.wait_ge(S["table_step"], 5 * r + 4)
                V.tensor_tensor(sidx[:, :], tmpi[:, 0, :], tabs[:, 1, :], ALU.add).then_inc(S["idx_ready"], 1)
                V.tensor_scalar(rkj, rkj, -float(SLOT_ROWS), None, ALU.add).then_inc(S["table_step"], 1)
                dve.wait_ge(S["table_step"], 5 * r + 5)

            V.sem_inc(S["y_ready"], 1)

            tables(0)
            bank = side.wait_full(dve, "count")
            side.was_read(V.tensor_reduce(cnt[:, 0:1], bank[:, 0:NE], AX.X, ALU.max), "count")
            side.wait_read(dve, "count")
            V.tensor_copy(maxu[:, :], cnt[:, 0:1]).then_inc(S["rank_ready"], 1)
            dve.wait_ge(S["exp_done"], 2)
            step(V.tensor_reduce(rv[:, 4, :], gtmp[:, :, :], AX.X, ALU.add))
            step(V.tensor_scalar_add(rv[:, 5, :], rv[:, 3, :], 1.0))
            step(V.tensor_tensor(rv[:, 4, :], rv[:, 4, :], rv[:, 5, :], ALU.mult))
            step(V.reciprocal(wk[:, 0, :], rv[:, 4, :]))
            step(V.tensor_tensor(wk[:, 1, :], wk[:, 0, :], rv[:, 3, :], ALU.mult))

            def experts(r):
                if not isinstance(r, int):
                    tables(r)
                    settle(dve)

                def turns(it):
                    for s in range(NSLOT):
                        n = r * NE + it * NSLOT + s
                        dve.wait_ge(S["silu_ready"], n + 1)
                        V.tensor_tensor(hid, sg, banks[5][:, P:2 * P], ALU.mult).then_inc(S["hid_ready"], 1)
                        dve.wait_ge(S["hT_full"], n + 1)
                        V.tensor_copy(hidT, banks[1][:, 0:P]).then_inc(S["hT_ready"], 1)
                        dve.wait_ge(S["y_full"], n + 1)
                        settle(dve)
                        if not first(r, it):
                            dve.wait_ge(scattered[s], (r * TURNS + it) * 16)
                        V.tensor_copy(Yo[:, s, :], banks[6][:, :]).then_inc(S["y_ready"], 1)

                if isinstance(r, int):
                    turns(0)
                    with dve.Fori(1, TURNS) as it:
                        turns(it)
                else:
                    with dve.Fori(0, TURNS) as it:
                        turns(it)

            experts(0)
            overflow(dve, experts)

            dve.wait_ge(S["ln2_in"], 32)

            def pairs(i):
                dve.wait_ge(S["scaled"], i + 1)
                tell(V.scalar_tensor_tensor(fin(i, 0), fin(i, 1), wk[:, 1, i:i + 1], fin(i, 0), ALU.mult, ALU.add),
                     "paired")

            def finish(i):
                f = fin(i, 0)
                dve.wait_ge(S["gated2"], i + 1)
                step(V.scalar_tensor_tensor(f, x1(i), ALPHA, f, ALU.mult, ALU.add))
                tell(norm_affine(f, f, ln2(0), ln2(1)), "out_ready")

            pairs(0)
            pairs(1)
            finish(0)
            pairs(2)
            finish(1)
            finish(2)

        @block.scalar
        def _(act):
            A_ = nc.scalar.activation
            act.dma_start(cond[:, 0, :], T["c"][0].rearrange("(p k) -> p k", k=KT)).then_inc(S["cond_in"], 16)
            act.dma_start(cond[:, 1, :], T["c_ctx"].rearrange("(p k) -> p k", k=KT)).then_inc(S["cond_in"], 16)
            act.wait_ge(S["zeros_set"], 3)

            def bias_rows(n):
                act.dma_start(abias[0:2, n % 2, :],
                              T["b_ada"][0:1, n * HALF:(n + 1) * HALF].to_broadcast([2, HALF])).then_inc(b_in[n % 2], 16)

            def ada_block(n):
                act.dma_start(adabuf.rearrange("p (k n) -> p k n", k=KT),
                              T["w_ada"][0].rearrange("(p k) n -> p k n", k=KT)[:, :, n * HALF:(n + 1) * HALF])\
                    .then_inc(S["ada_in"], 16)

            bias_rows(0)
            bias_rows(1)
            act.wait_ge(S["cond_in"], 32)
            A_(conde[:, :, :], cond[:, :, :], ACT.Exp, scale=-1.0).then_inc(S["cond_exp"], 1)
            for n in (2, 3):
                main.wait_read(act, "ada", n - 2)
                bias_rows(n)
            for n in (4, 5):
                main.wait_read(act, "ada", n - 2)
                bias_rows(n)
            ada_block(4)
            side.wait_read(act, "modc", 0)
            for i in range(TILES):
                bank = side.wait_full(act, "xT", i, 0)
                for k in range(4):
                    ins = A_(hT[:, i, k, :], bank[:, k * P:(k + 1) * P], ACT.Identity,
                             scale=modc[:, KT + k, stream(i):stream(i) + 1],
                             bias=modc[:, k, stream(i):stream(i) + 1])
                side.was_read(ins, "xT", i, 0)
            exps = [0]
            for j, (kind, n, i) in enumerate(PROJ):
                bank = main.wait_full(act, "proj", kind, n, i)
                dst = {"kvl": lambda: kvl[:, i, :], "gqk": lambda: gqk[:, i].rearrange("p a b -> p (a b)"),
                       "vg": lambda: vg[:, i, :], "q": lambda: q[:, i, :], "rg": lambda: rg[:, i, :],
                       "mg": lambda: mgs[:, i, n // 2, (n % 2) * HALF:(n % 2 + 1) * HALF]}[kind]()
                main.was_read(A_(dst, bank[:, 0:dst.shape[1]], ACT.Copy), "proj", kind, n, i)
                for what, a in AFTER[j]:
                    if what == "rows":
                        main.wait_read(act, "ada", a)
                        if a + 2 < 12:
                            bias_rows(a + 2)
                    elif what == "lr":
                        bank = side.wait_full(act, "lr", a)
                        side.was_read(A_(lrT[:, a * P:(a + 1) * P], bank[0:2 * RANK, 0:P], ACT.Copy), "lr", a)
                    elif what == "z":
                        act.wait_ge(S["z_ready"], a + 1)
                        zz = kl[:, a].rearrange("p d n -> p (d n)")
                        A_(zz, zz, ACT.Exp).then_inc(S["lexp"], 1)
                        act.wait_ge(S["lexp"], 2 * a + 1)
                        A_(zz, zz, ACT.Ln, bias=1.0).then_inc(S["lexp"], 1)
                    elif what == "cum":
                        if a:
                            act.wait_ge(S["qk_decayed"], a)
                        bank = side.wait_full(act, "cum", a)
                        flat = [E[:, j2].rearrange("p d n -> p (d n)") for j2 in range(3)]
                        A_(flat[0], bank[:, :], ACT.Exp)
                        side.was_read(A_(flat[1], bank[:, :], ACT.Exp, scale=-1.0), "cum", a)
                        bank = side.wait_full(act, "rest", a)
                        side.was_read(A_(flat[2], bank[:, :], ACT.Exp), "rest", a)
                        bank = side.wait_full(act, "decay", a)
                        side.was_read(A_(decay[:, a, :], bank[:, 0:8], ACT.Exp), "decay", a)
                    elif what == "tr":
                        bank = side.wait_full(act, "qgT", a)
                        side.was_read(A_(qgT[:, a].rearrange("p j t -> p (j t)"), bank[:, :], ACT.Copy), "qgT", a)
                    elif what == "at":
                        if a:
                            act.wait_ge(S["intra_done"], a)
                        for d in range(2):
                            bank = side.wait_full(act, "at", a, d)
                            b4 = bank[:, :].rearrange("p (h t) -> p h t", h=GH)
                            for c in range(2):
                                rows = slice(c * CHUNK, (c + 1) * CHUNK)
                                ins = A_(A[rows, d, :, rows], b4[rows, :, rows], ACT.Copy)
                            side.was_read(ins, "at", a, d)
                    elif what == "qT":
                        bank = side.wait_full(act, "qT", a)
                        side.was_read(A_(qT[:, a].rearrange("p j t -> p (j t)"), bank[:, :], ACT.Copy), "qT", a)
                    elif what == "gout":
                        main.wait_read(act, "proj", "rg", 0, a)
                        act.wait_ge(S["qk_decayed"], TILES)
                        A_(E[:, a].rearrange("p d n -> p (d n)"), rg[:, a, :], ACT.Exp, scale=-1.0)\
                            .then_inc(S["gout_exp"], 1)
                    elif what == "gT":
                        bank = side.wait_full(act, "gT", a)
                        side.was_read(A_(glaT[:, a].rearrange("p k t -> p (k t)"), bank[:, :], ACT.Copy), "gT", a)
                    elif what == "score":
                        ti, h = HEAD_JOBS[a]
                        w = 3 * P if ti < LAT_TILES else P
                        act.wait_ge(S["negmax_ready"], a + 1)
                        if a >= 4:
                            side.wait_full(act, "pT", a - 4)
                        bank = side.bank("score", a)
                        ins = A_(Pr[:, a % 4, 0:w], bank[:, 0:w], ACT.Exp, bias=negmax[:, a % 3:a % 3 + 1],
                                 accum_out=rowsum[:, ti, h:h + 1])
                        side.was_read(ins, "score", a)
                for what, a in AFTER[j]:
                    if what == "rows":
                        side.wait_read(act, "rows", a)
                        if a > 4:
                            act.wait_ge(S["mod_stored"], 16 * (a - 4))
                        act.dma_start(mod_d[:, (a - 4) * HALF:(a - 3) * HALF], part[0:2, a % 4, :])\
                            .then_inc(S["mod_stored"], 16)
                    elif what == "ada":
                        main.wait_full(act, "ada", a)
                        if a < 11:
                            ada_block(a + 1)
            for i in (2, 0, 1):
                bank = side.wait_full(act, "aT", i)
                side.was_read(A_(attnT[:, i].rearrange("p k t -> p (k t)"), bank[:, :], ACT.Copy), "aT", i)
            for i in range(TILES):
                main.wait_read(act, "proj", "mg", 3, i)
                m = mgs[:, i].rearrange("p m n -> p (m n)")
                A_(m, m, ACT.Sigmoid).then_inc(S["mg_sig"], 1)
            act.wait_ge(S["pv_done"], len(HEAD_JOBS))
            act.wait_ge(S["gated"], TILES)
            act.wait_ge(S["mod_stored"], 16 * 8)
            for dst, n in ((g1b, 4), (sc2b, 8), (sh2b, 6)):
                for st in range(2):
                    act.dma_start(dst[:, st, :], mod_d[st:st + 1, (n - 4) * HALF:(n - 2) * HALF].to_broadcast([P, D]))\
                        .then_inc(S["mod_in"], 16)
            for i in range(TILES):
                for g in range(2):
                    bank = side.wait_full(act, "mT", i, g)
                    side.was_read(A_(mT[:, i, 4 * g:4 * g + 4, :].rearrange("p k t -> p (k t)"), bank[:, :], ACT.Copy),
                                  "mT", i, g)
                if i == 1:
                    main.wait_full(act, "br", 1, TILES - 1, 1)
                    for t in range(TILES):
                        src = T["x_sample"][0, t * P:(t + 1) * P, :] if t < LAT_TILES else T["x_prompt"][0]
                        act.dma_start(xr(t), src).then_inc(xr_in[t], 16)
                if i < 2:
                    act.dma_start(ln1(i), (T["ln1_g"], T["ln1_b"])[i].to_broadcast([P, D])).then_inc(S["ln1_in"], 16)
            for i in range(TILES):
                for g in range(2):
                    bank = side.wait_full(act, "hT", i, g)
                    side.was_read(A_(h2T[:, i, 4 * g:4 * g + 4, :].rearrange("p k t -> p (k t)"), bank[:, :], ACT.Copy),
                                  "hT", i, g)
            act.wait_ge(S["h2_ready"], TILES)
            for j in range(2):
                act.dma_start(ln2(j), (T["ln2_g"], T["ln2_b"])[j].to_broadcast([P, D])).then_inc(S["ln2_in"], 16)
            act.wait_ge(S["exp_asked"], 1)
            A_(gtmp[:, :, :], gtmp[:, :, :], ACT.Exp).then_inc(S["exp_done"], 1)
            act.wait_ge(S["exp_asked"], 2)
            A_(rv[:, 3, :], rv[:, 3, :], ACT.Exp).then_inc(S["exp_done"], 1)

            def tokens(b):
                A_(xTe[:, b].rearrange("p k n -> p (k n)"), banks[0][:, :], ACT.Copy).then_inc(S["xTe_ready"], 1)

            def experts(r):
                act.wait_ge(S["xTe_full"], r * (NE + 1) + 1)
                tokens(0)
                with act.Fori(0, TURNS) as it:
                    for s in range(NSLOT):
                        n = it * NSLOT + s
                        act.wait_ge(S["gu_full"], r * NE + n + 1)
                        A_(sg, banks[5][:, 0:P], ACT.Silu).then_inc(S["silu_ready"], 1)
                        act.wait_ge(S["xTe_full"], r * (NE + 1) + n + 2)
                        tokens((s + 1) % 2)

            experts(0)
            overflow(act, experts)
            for i in range(TILES):
                act.wait_ge(fin_in[i], 32)
                A_(fin(i, 0), fin(i, 0), ACT.Copy, scale=wk[:, 0, i:i + 1]).then_inc(S["scaled"], 1)

        @block.tensor
        def _(pe):
            mm, tp = nc.tensor.matmul, nc.tensor.transpose

            def weights(*w):
                j = WJ[w]
                pe.wait_ge(w_in[j % 2], WCOUNT[w])
                return W[:, j % 2, :]

            def used(ins, *w):
                ins.then_inc(w_free[WJ[w] % 2], 1)

            def modulation(n):
                if n < 4:
                    w = weights("ada", n)
                else:
                    w = adabuf
                    pe.wait_ge(S["ada_in"], 16 * (n - 3))
                w = w.rearrange("p (k n) -> p k n", k=KT)
                bank = main.claim(pe, "ada", n)
                for k in range(KT):
                    j = k % 4
                    ins = mm(bank[32 * j:32 * j + 32, :], csil[:, k, :], w[:, k, :], start=k < 4, stop=k >= 4,
                             skip_group_check=True)
                main.filled(ins, "ada", n)
                if n < 4:
                    main.wait_full(pe, "ada", n)
                    used(pe.nop(), "ada", n)

            def columns(bank, at, n):
                main.wait_read(pe, "ada", n)
                for j in range(4):
                    ins = mm(bank[:, at + 2 * j:at + 2 * j + 2], part[:, n % 4, j * P:(j + 1) * P], const("selcol"),
                             start=True, stop=True)
                return ins

            pe.wait_ge(S["consts_in"], 16)
            pe.wait_ge(S["cond_silu"], 2)
            colbank = side.claim(pe, "modc", 0)
            for n in range(4):
                modulation(n)
                if n:
                    columns(colbank, 8 * (n - 1), n - 1)

            def x_transposes(i, g):
                if g == 0:
                    pe.wait_ge(S["x_normed"], i + 1)
                bank = side.claim(pe, "xT", i, g)
                for j in range(4):
                    k = 4 * g + j
                    ins = tp(bank[:, j * P:(j + 1) * P], x[:, i, k * P:(k + 1) * P], ident)
                side.filled(ins, "xT", i, g)

            x_transposes(0, 0)
            x_transposes(0, 1)
            side.filled(columns(colbank, 24, 3), "modc", 0)
            for i in (1, 2):
                for g in range(2):
                    x_transposes(i, g)

            def project(kind, n, i):
                w = weights(kind, n)
                cols = KVL if kind == "kvl" else HALF
                w = w[:, 0:KT * cols].rearrange("p (k n) -> p k n", k=KT)
                if kind == "kvl":
                    for g in range(2):
                        side.wait_read(pe, "xT", i, g)
                bank = main.claim(pe, "proj", kind, n, i)
                for k in range(KT):
                    ins = mm(bank[:, 0:cols], hT[:, i, k, :], w[:, k, :], start=k == 0, stop=k == KT - 1)
                main.filled(ins, "proj", kind, n, i)
                if i == TILES - 1:
                    main.wait_full(pe, "proj", kind, n, i)
                    used(pe.nop(), kind, n)

            def intra(a):
                pe.wait_ge(S["at_masked"], 2 * a + 2)
                if a == 0:
                    main.wait_read(pe, "proj", "vg", 0, TILES - 1)
                for d in range(2):
                    for h in range(GH):
                        ins = mm(outb[a][:, h * DV:(h + 1) * DV], A[:, d, h, :], vg[:, a, h * DV:(h + 1) * DV],
                                 start=d == 0 and h == 0, stop=False, skip_group_check=True)
                ins.then_inc(S["intra_done"], 1)

            def chain(lat, a):
                St, name = (Sl, "uL") if lat else (Sc, "uC")
                where = []
                for d in range(2):
                    c = a if d == 0 else (3 if lat else 1) - a
                    where.append((c // 2, c % 2) if lat else (CTX, c))
                if lat and a == 0:
                    pe.wait_ge(S["states_in"], 64)
                if a:
                    for d in range(2):
                        side.wait_read(pe, name, a - 1, d)
                if lat or a:
                    for d, (tile, c) in enumerate(where):
                        for pr in range(PAIRS):
                            rows = slice(c * CHUNK, (c + 1) * CHUNK)
                            ins = mm(outb[tile][rows, pr * 2 * DV:(pr + 1) * 2 * DV], qgT[:, tile, 2 * d + pr, rows],
                                     St[:, d, pr, :], start=False, stop=False, skip_group_check=True)
                    if (lat and a == 3) or not lat:
                        ins.then_inc(S["gla_full"], 1)
                if lat and a == 3:
                    return
                for d, (tile, c) in enumerate(where):
                    bank = side.claim(pe, name, a, d)
                    for pr in range(PAIRS):
                        rows = slice(c * CHUNK, (c + 1) * CHUNK)
                        for hh in range(2):
                            h = 2 * pr + hh
                            ins = mm(bank[hh * DK:(hh + 1) * DK, h * DV:(h + 1) * DV],
                                     kl[rows, tile, d, h * DK:(h + 1) * DK], vg[rows, tile, h * DV:(h + 1) * DV],
                                     start=True, stop=True, skip_group_check=True)
                    side.filled(ins, name, a, d)

            def four(job, src):
                bank = side.claim(pe, *job)
                for j in range(4):
                    ins = tp(bank[:, j * P:(j + 1) * P], src(j), ident)
                side.filled(ins, *job)

            gla_order = {2: 1, 0: 2, 1: 3}
            for j, (kind, n, i) in enumerate(PROJ):
                project(kind, n, i)
                for what, a in AFTER[j]:
                    if what == "ada":
                        modulation(a)
                    elif what == "rows":
                        bank = side.claim(pe, "rows", a)
                        main.wait_read(pe, "ada", a)
                        side.filled(mm(bank[0:2, :], const("selcol"), part[:, a % 4, :], start=True, stop=True),
                                    "rows", a)
                    elif what == "lr":
                        if a == 0:
                            pe.wait_ge(S["small_in"], 16 * 5)
                        main.wait_read(pe, "proj", "kvl", 0, a)
                        bank = side.claim(pe, "lr", a)
                        side.filled(tp(bank[0:2 * RANK, 0:P], kvl[:, a, 2 * KV * HD:KVL], ident), "lr", a)
                    elif what == "z":
                        side.wait_read(pe, "lr", a)
                        bank = side.claim(pe, "z", a)
                        side.filled(mm(bank[:, :], lrT[:, a * P:(a + 1) * P], wgate2[0:2 * RANK, :], start=True, stop=True),
                                    "z", a)
                    elif what == "cum":
                        pe.wait_ge(S["logg_ready"], a + 1)
                        for job, m in (("cum", "incl"), ("rest", "excl")):
                            bank = side.claim(pe, job, a)
                            for d, x_ in enumerate("fb"):
                                ins = mm(bank[:, d * GH * DK:(d + 1) * GH * DK], const(f"{m}_{x_}"), logg[:, a, d, :],
                                         start=True, stop=True)
                            side.filled(ins, job, a)
                        bank = side.claim(pe, "decay", a)
                        for d in range(2):
                            for pr in range(PAIRS):
                                c = 4 * d + 2 * pr
                                ins = mm(bank[:, c:c + 2], logg[:, a, d, pr * P:(pr + 1) * P], const("chunks"),
                                         start=True, stop=True)
                        side.filled(ins, "decay", a)
                    elif what == "tr":
                        pe.wait_ge(S["qk_decayed"], a + 1)
                        for job, m in (("qgT", 0), ("kgT", 1)):
                            four((job, a), lambda jj: qkt[:, m, jj // 2, (jj % 2) * P:(jj % 2 + 1) * P])
                    elif what == "at":
                        side.wait_read(pe, "qgT", a)
                        side.wait_read(pe, "kgT", a)
                        for d in range(2):
                            bank = side.claim(pe, "at", a, d)
                            for h in range(GH):
                                jj = 2 * d + h // 2
                                ins = mm(bank[:, h * P:(h + 1) * P], kgz[:, jj, h % 2, :], qgT[:, a, jj, :],
                                         start=True, stop=True)
                            side.filled(ins, "at", a, d)
                    elif what == "intra":
                        intra(a)
                    elif what in ("chainL", "chainC"):
                        chain(what == "chainL", a)
                    elif what == "kT":
                        if a < TILES:
                            pe.wait_ge(S["kprepped"], a + 1)
                        bank = side.claim(pe, "kT", a)
                        side.filled(tp(bank[:, 0:P], kvl[:, a, 0:KV * HD] if a < TILES else kc, ident), "kT", a)
                    elif what == "qT":
                        pe.wait_ge(S["q_ready"], a + 1)
                        four(("qT", a), lambda jj: q[:, a, jj * P:(jj + 1) * P])
                    elif what == "gT":
                        pe.wait_ge(S["gated"], gla_order[a])
                        four(("gT", a), lambda jj: rg[:, a, jj * P:(jj + 1) * P])
                    elif what == "score":
                        ti, h = HEAD_JOBS[a]
                        if h == 0:
                            side.wait_read(pe, "qT", ti)
                            side.wait_read(pe, "kT", 2)
                            side.wait_read(pe, "kT", 3)
                        bank = side.claim(pe, "score", a)
                        keys = kTl[:, h // 4, :] if ti < LAT_TILES else kTc[:, h // 4, :]
                        side.filled(mm(bank[:, 0:keys.shape[1]], qT[:, ti, h % 4, :], keys, start=True, stop=True),
                                    "score", a)
                    elif what == "pT":
                        ti, h = HEAD_JOBS[a]
                        side.wait_read(pe, "score", a)
                        bank = side.claim(pe, "pT", a)
                        for c in range(3 if ti < LAT_TILES else 1):
                            ins = tp(bank[:, c * P:(c + 1) * P], Pr[:, a % 4, c * P:(c + 1) * P], ident)
                        side.filled(ins, "pT", a)
                    elif what == "pv":
                        ti, h = HEAD_JOBS[a]
                        side.wait_read(pe, "pT", a)
                        if h == 0:
                            pe.wait_ge(S["gla_read"], gla_order[ti])
                        vcols = slice(KV * HD + (h // 4) * HD, KV * HD + (h // 4 + 1) * HD)
                        vals = [kvl[:, 0, vcols], kvl[:, 1, vcols], vc[:, (h // 4) * HD:(h // 4 + 1) * HD]] \
                            if ti < LAT_TILES else [kvl[:, CTX, vcols]]
                        for c, v in enumerate(vals):
                            ins = mm(outb[ti][:, h * HD:(h + 1) * HD], PTr[:, a % 4, c * P:(c + 1) * P], v,
                                     start=c == 0, stop=c == len(vals) - 1)
                        ins.then_inc(S["pv_done"], 1)
            for m, i in enumerate((2, 0, 1)):
                pe.wait_ge(S["att_normed"], m + 1)
                four(("aT", i), lambda jj: q[:, i, jj * P:(jj + 1) * P])

            def merged_transposes(i):
                pe.wait_ge(S["merged_ready"], TILES + i + 1)
                for g in range(2):
                    four(("mT", i, g), lambda jj: merged(i)[:, (4 * g + jj) * P:(4 * g + jj + 1) * P])

            for n in range(2):
                w = weights("br", n).rearrange("p (m k n) -> p m k n", m=2, k=4)
                for i in range(TILES):
                    if n == 0:
                        side.wait_read(pe, "aT", i)
                        side.wait_read(pe, "gT", i)
                    for m, src in enumerate((attnT, glaT)):
                        if n == 1 and i > 0 and m == 1:
                            merged_transposes(i - 1)
                        bank = main.claim(pe, "br", n, i, m)
                        for k in range(4):
                            ins = mm(bank[:, :], src[:, i, k, :], w[:, m, k, :], start=k == 0, stop=k == 3)
                        main.filled(ins, "br", n, i, m)
                main.wait_full(pe, "br", n, TILES - 1, 1)
                used(pe.nop(), "br", n)
            for i in range(TILES):
                if i == 1:
                    merged_transposes(TILES - 1)
                for g in range(2):
                    side.wait_read(pe, "mT", i, g)
                for n in range(2):
                    w = weights("wo", n).rearrange("p (k n) -> p k n", k=KT)
                    bank = main.claim(pe, "wo", n, i)
                    for k in range(KT):
                        ins = mm(bank[:, :], mT[:, i, k, :], w[:, k, :], start=k == 0, stop=k == KT - 1)
                    main.filled(ins, "wo", n, i)
                    if i == TILES - 1:
                        main.wait_full(pe, "wo", n, i)
                        used(pe.nop(), "wo", n)

            def second_transposes(i):
                pe.wait_ge(S["h2_ready"], i + 1)
                for g in range(2):
                    four(("hT", i, g), lambda jj: xr(i)[:, (4 * g + jj) * P:(4 * g + jj + 1) * P])

            for i in range(TILES):
                second_transposes(i)
                if i == 0:
                    bank = main.claim(pe, "router")
                for g in range(2):
                    side.wait_read(pe, "hT", i, g)
                    for k in range(4 * g, 4 * g + 4):
                        ins = mm(bank[:, i * (GROUPS + NE):(i + 1) * (GROUPS + NE)], h2T[:, i, k, :],
                                 wrouter[:, k, :], start=k == 0, stop=k == KT - 1, skip_group_check=True)
            main.filled(ins, "router")
            pe.wait_ge(S["both_ready"], 1)
            bank = side.claim(pe, "rank")
            flat = both[:, :, :].rearrange("p i n -> p (i n)")
            mm(bank[:, 0:TILES * NE], const("before"), flat, start=True, stop=True, skip_group_check=True)
            for i in range(1, TILES):
                ins = mm(bank[:, i * NE:TILES * NE], const("ones"), flat[:, 0:(TILES - i) * NE], start=False, stop=True,
                         skip_group_check=True)
            side.filled(ins, "rank")
            bank = side.claim(pe, "count")
            for i in range(TILES):
                ins = mm(bank[:, 0:NE], const("ones"), both[:, i, :], start=i == 0, stop=i == TILES - 1)
            side.filled(ins, "count")
            main.wait_read(pe, "wo", 0, TILES - 1)
            main.wait_read(pe, "wo", 1, TILES - 1)
            main.wait_read(pe, "router")

            def tokens(b):
                g = G[:, b, :].rearrange("p (q c) -> p q c", c=4)
                for c in range(4):
                    ins = tp(banks[0][:, c * P:(c + 1) * P], g[:, :, c], ident)
                ins.then_inc(S["xTe_full"], 1)

            def experts(r):
                pe.wait_ge(S["onehot_ready"], r + 1)
                for j in range(TOPK * TILES):
                    ins = mm(banks[4][:, 0:2 * NE], Rk[j], idr[:, j].rearrange("p c n -> p (c n)"),
                             start=j == 0, stop=j == TOPK * TILES - 1)
                ins.then_inc(S["tables_full"], 1)
                pe.wait_ge(g_in[0], (r * (TURNS + 1) + 1) * 16)
                tokens(0)
                def turns(it):
                    for s in range(NSLOT):
                        n = it * NSLOT + s
                        own = isinstance(it, int) and s in OWN
                        w = OWN[s] if own else s
                        x_, (wg, wu), wd = xTe[:, s % 2], ebuf[w][0], ebuf[w][1]
                        if own:
                            pe.wait_ge(ew_in[w], 32)
                        else:
                            pe.wait_ge(ew_in[s], (r * slot_turns(s) + it + 1 - (s in OWN)) * 32)
                        pe.wait_ge(S["xTe_ready"], r * (NE + 1) + n + 1)
                        for k in range(KT):
                            h, c = k // 4, k % 4
                            if w < len(egu):
                                parts = [(0, 2 * P, lambda hh: egu[w][:, :, k, hh * P:(hh + 1) * P])]
                            else:
                                parts = [(0, P, lambda hh: wg[:, k, hh * P:(hh + 1) * P]),
                                         (P, 2 * P, lambda hh: wu[:, k, hh * P:(hh + 1) * P])]
                            for a, b, rhs in parts:
                                for hh in range(2):
                                    ins = mm(banks[5][hh * 64:hh * 64 + 64, a:b], x_[:, c, h * 64:h * 64 + 64],
                                             rhs(hh), start=k == 0 and a == 0, stop=k == KT - 1,
                                             skip_group_check=True)
                        ins.then_inc(S["gu_full"], 1)
                        pe.wait_ge(g_in[(s + 1) % NSLOT], (r * (TURNS + 1) + it + 1 + (s + 1) // NSLOT) * 16)
                        tokens((s + 1) % NSLOT)
                        pe.wait_ge(S["hid_ready"], r * NE + n + 1)
                        tp(banks[1][:, 0:P], hid, ident).then_inc(S["hT_full"], 1)
                        pe.wait_ge(S["hT_ready"], r * NE + n + 1)
                        pe.wait_ge(S["y_ready"], r * NE + n + 1)
                        if own:
                            pe.wait_ge(ed_in[w], 32 if w == PARTED else 16)
                        else:
                            pe.wait_ge(ed_in[s], (r * slot_turns(s) + it + 1 - (s in OWN)) * 16)
                        for hh in range(2):
                            for o in range(2):
                                ins = mm(banks[6][o * 64:o * 64 + 64, :], hidT[:, hh * 64:hh * 64 + 64],
                                         wd[hh][:, o * HALF:(o + 1) * HALF], start=hh == 0, stop=hh == 1,
                                         skip_group_check=True)
                        ins.then_inc(S["y_full"], 1)
                        if not own:
                            pe.wait_ge(S["y_full"], r * NE + n + 1)
                            pe.nop().then_inc(ew_free[s], 1)

                turns(0)
                with pe.Fori(1, TURNS) as it:
                    turns(it)

            experts(0)
            overflow(pe, experts)
            pe.nop().then_inc(S["slots_done"], 1)


_INS = ["x_prompt", "x_sample", "cache_k", "cache_v", "state_gla_fwd", "state_gla_bwd", "c", "c_ctx", "w_ada",
        "b_ada", "w_in", "q_norm", "k_norm", "gla_w_gate", "gla_b_gate", "gla_norm", "w_br_attn", "w_br_gla",
        "w_out", "ln1_g", "ln1_b", "router_group_w", "router_group_b", "router_expert_w", "router_expert_b",
        "exp_w_gate", "exp_w_up", "exp_w_down", "ln2_g", "ln2_b"]
_OUTS = [("o_prompt", (1, N_CTX, D)), ("o_sample", (1, N_LAT, D)), ("o_k", (1, 1, N_CTX, KV, HD)),
         ("o_v", (1, 1, N_CTX, KV, HD)), ("o_sf", (1, 1, GH, DK, DV)), ("o_sb", (1, 1, GH, DK, DV))]


def kernel(**inputs):
    import concourse.bacc as _bacc
    from concourse.bass_utils import run_bass_kernel_spmd as _run

    nc = _bacc.Bacc("TRN2", target_bir_lowering=False, num_devices=1)
    arrays = {n: np.ascontiguousarray(inputs[n]) for n in _INS}
    arrays["consts"] = constants()
    tensors = {n: nc.dram_tensor(n, a.shape, fp32, kind="ExternalInput").ap() for n, a in arrays.items()}
    for n, shape in _OUTS:
        tensors[n] = nc.dram_tensor(n, shape, fp32, kind="ExternalOutput").ap()
    program(nc, tensors)
    r = _run(nc, [arrays], core_ids=[0])
    return tuple(r.results[0][n] for n, _ in _OUTS)
```
